# Optimizing a Trainium2 kernel written in Bass

```python
import jax, jax.numpy as jnp
from jax import lax
import numpy as np

D_MODEL = 1024
BATCH = 1
SEQ = 1024
DEPTH = 1

N_MEM = 256
ML_HEADS = 4
ML_DIM = 1024
ML_HEAD_DIM = ML_DIM // ML_HEADS
ML_CHUNK = 128
HG_EXPAND = 128
HG_DIM = 1024
HG_HEADS = HG_DIM // HG_EXPAND
HG_VDIM = HG_DIM // HG_HEADS
HG_CHUNK = 64
X_HEADS = 4
X_HEAD_DIM = D_MODEL // X_HEADS
D_FF = 2816
CONV_W = 3
EPS = 1e-6
IN_SPLITS = (2 * ML_DIM, ML_DIM, ML_DIM, 4 * ML_HEADS,
             HG_DIM, HG_DIM, HG_DIM, HG_DIM, HG_DIM,
             D_MODEL, D_MODEL)
IN_DIM = 4 * ML_DIM + 4 * ML_HEADS + 5 * HG_DIM + 2 * D_MODEL

kernel_name = "hybrid_mlstm_hgrn2_gated_merge_encoder"

def rmsnorm(x, g):
    xf = x.astype(jnp.float32)
    y = xf * lax.rsqrt(jnp.mean(xf * xf, axis=-1, keepdims=True) + EPS)
    return (y * g.astype(jnp.float32)).astype(x.dtype)

def dwconv(x, w, b):
    c = x.shape[-1]
    k = w.shape[0]
    y = lax.conv_general_dilated(x, w[:, None, :].astype(x.dtype), window_strides=(1,),
                                 padding=[(k // 2, k // 2)],
                                 dimension_numbers=('NWC', 'WIO', 'NWC'),
                                 feature_group_count=c)
    return y + b.astype(x.dtype)

def to_heads(t, h):
    b, s, c = t.shape
    return t.reshape(b, s, h, c // h).transpose(0, 2, 1, 3)

def head_rmsnorm(t, g):
    b, h, s, d = t.shape
    t = t.transpose(0, 2, 1, 3)
    y = t * lax.rsqrt(jnp.mean(t * t, axis=-1, keepdims=True) + EPS)
    return y.reshape(b, s, h * d) * g.astype(jnp.float32)

def split_cols(t, sizes):
    out, o = [], 0
    for n in sizes:
        out.append(t[..., o:o + n])
        o += n
    return out

def to_chunks(t, l):
    nc = t.shape[2] // l
    return jnp.moveaxis(t.reshape(t.shape[:2] + (nc, l) + t.shape[3:]), 2, 0)

def from_chunks(t):
    t = jnp.moveaxis(t, 0, 2)
    return t.reshape(t.shape[:2] + (t.shape[2] * t.shape[3],) + t.shape[4:])

def mlstm_scan(q, k, v, log_i, log_f):
    b_, h_, s_, d = q.shape
    l = ML_CHUNK
    causal = jnp.tril(jnp.ones((l, l), dtype=bool))

    def step(carry, inp):
        c_st, n_st, m_st = carry
        qc, kc, vc, ic, fc = inp
        bcum = jnp.cumsum(fc, axis=-1)
        log_d = jnp.where(causal, bcum[..., :, None] - bcum[..., None, :] + ic[..., None, :], -jnp.inf)
        m_inter = bcum + m_st[..., None]
        m_t = jnp.maximum(m_inter, jnp.max(log_d, axis=-1))
        dmat = jnp.exp(log_d - m_t[..., None])
        sc = jnp.einsum('bhtd,bhsd->bhts', qc, kc) * dmat
        w_inter = jnp.exp(m_inter - m_t)
        num = jnp.einsum('bhts,bhsv->bhtv', sc, vc) + w_inter[..., None] * jnp.einsum('bhtk,bhkv->bhtv', qc, c_st)
        den = jnp.sum(sc, axis=-1) + w_inter * jnp.einsum('bhtk,bhk->bht', qc, n_st)
        hc = num / jnp.maximum(jnp.abs(den), jnp.exp(-m_t))[..., None]
        g_end = bcum[..., -1]
        log_w = g_end[..., None] - bcum + ic
        m_new = jnp.maximum(g_end + m_st, jnp.max(log_w, axis=-1))
        wgt = jnp.exp(log_w - m_new[..., None])
        decay = jnp.exp(g_end + m_st - m_new)
        c_new = decay[..., None, None] * c_st + jnp.einsum('bhs,bhsk,bhsv->bhkv', wgt, kc, vc)
        n_new = decay[..., None] * n_st + jnp.einsum('bhs,bhsk->bhk', wgt, kc)
        return (c_new, n_new, m_new), hc

    init = (jnp.zeros((b_, h_, d, d), jnp.float32), jnp.zeros((b_, h_, d), jnp.float32),
            jnp.zeros((b_, h_), jnp.float32))
    xs = (to_chunks(q, l), to_chunks(k, l), to_chunks(v, l), to_chunks(log_i, l), to_chunks(log_f, l))
    _, hs = lax.scan(step, init, xs)
    return from_chunks(hs)

def hgrn2_scan(q, k, v, log_f):
    b_, h_, s_, dk = q.shape
    dv = v.shape[-1]
    l = HG_CHUNK
    causal = jnp.tril(jnp.ones((l, l), dtype=bool))[:, :, None]

    def step(s_st, inp):
        qc, kc, vc, fc = inp
        bcum = jnp.cumsum(fc, axis=-2)
        rel = bcum[:, :, :, None, :] - bcum[:, :, None, :, :]
        dec = jnp.exp(jnp.where(causal, rel, -jnp.inf))
        att = jnp.einsum('bhtk,bhtsk,bhsk->bhts', qc, dec, kc)
        oc = jnp.einsum('bhts,bhsv->bhtv', att, vc) + jnp.einsum('bhtk,bhkv->bhtv', qc * jnp.exp(bcum), s_st)
        b_end = bcum[:, :, -1]
        kd = kc * jnp.exp(b_end[:, :, None] - bcum)
        s_new = jnp.exp(b_end)[..., None] * s_st + jnp.einsum('bhsk,bhsv->bhkv', kd, vc)
        return s_new, oc

    init = jnp.zeros((b_, h_, dk, dv), jnp.float32)
    xs = (to_chunks(q, l), to_chunks(k, l), to_chunks(v, l), to_chunks(log_f, l))
    _, os_ = lax.scan(step, init, xs)
    return from_chunks(os_)

def flip(t):
    return jnp.flip(t, axis=2)

def setup_inputs(seed: int = 0) -> dict:
    key = jax.random.key(seed)
    ks = jax.random.split(key, 26)
    f32 = jnp.float32

    def nrm(k, shape, scale):
        return jax.random.normal(k, shape, f32) * scale

    def gain(k, shape):
        return 1.0 + 0.02 * jax.random.normal(k, shape, f32)

    fbias_mask = jnp.array([0.0, 1.0, 0.0, 1.0], f32)[:, None]
    ml_gate_b = (fbias_mask * jnp.linspace(3.0, 6.0, ML_HEADS, dtype=f32)[None, :])[None] \
        + nrm(ks[6], (DEPTH, 4, ML_HEADS), 0.1)
    return {
        "x": nrm(ks[0], (BATCH, SEQ, D_MODEL), 1.0),
        "mem": nrm(ks[1], (BATCH, N_MEM, D_MODEL), 1.0),
        "norm_mix_g": gain(ks[2], (DEPTH, D_MODEL)),
        "w_in": nrm(ks[3], (DEPTH, D_MODEL, IN_DIM), D_MODEL ** -0.5),
        "ml_conv_w": nrm(ks[4], (DEPTH, CONV_W, 2 * ML_DIM), CONV_W ** -0.5),
        "ml_conv_b": nrm(ks[5], (DEPTH, 2 * ML_DIM), 0.02),
        "ml_gate_b": ml_gate_b,
        "ml_norm_g": gain(ks[7], (DEPTH, ML_DIM)),
        "hg_lb": nrm(ks[8], (2, DEPTH + 1, HG_DIM), 0.1),
        "hg_norm_g": gain(ks[9], (DEPTH, HG_DIM)),
        "w_branch_m": nrm(ks[10], (DEPTH, ML_DIM, D_MODEL), ML_DIM ** -0.5),
        "w_branch_h": nrm(ks[11], (DEPTH, HG_DIM, D_MODEL), HG_DIM ** -0.5),
        "w_out": nrm(ks[12], (DEPTH, D_MODEL, D_MODEL), D_MODEL ** -0.5),
        "norm_x_g": gain(ks[13], (DEPTH, D_MODEL)),
        "norm_mem_g": gain(ks[14], (DEPTH, D_MODEL)),
        "w_q_x": nrm(ks[15], (DEPTH, D_MODEL, D_MODEL), D_MODEL ** -0.5),
        "w_kv_x": nrm(ks[16], (DEPTH, D_MODEL, 2 * D_MODEL), D_MODEL ** -0.5),
        "w_o_x": nrm(ks[17], (DEPTH, D_MODEL, D_MODEL), D_MODEL ** -0.5),
        "norm_ffn_g": gain(ks[18], (DEPTH, D_MODEL)),
        "w_up": nrm(ks[19], (DEPTH, D_MODEL, 2 * D_FF), D_MODEL ** -0.5),
        "ffn_conv_w": nrm(ks[20], (DEPTH, CONV_W, D_FF), CONV_W ** -0.5),
        "ffn_conv_b": nrm(ks[21], (DEPTH, D_FF), 0.02),
        "w_down": nrm(ks[22], (DEPTH, D_FF, D_MODEL), D_FF ** -0.5),
        "norm_final_g": gain(ks[23], (D_MODEL,)),
    }

def reference(x, mem, norm_mix_g, w_in, ml_conv_w, ml_conv_b, ml_gate_b, ml_norm_g, hg_lb,
              hg_norm_g, w_branch_m, w_branch_h, w_out, norm_x_g, norm_mem_g, w_q_x, w_kv_x,
              w_o_x, norm_ffn_g, w_up, ffn_conv_w, ffn_conv_b, w_down, norm_final_g):
    f32 = jnp.float32
    dt = x.dtype
    bsz, seq, _ = x.shape
    lb_all = jnp.cumsum(jax.nn.softmax(hg_lb.astype(f32), axis=1), axis=1)

    for l in range(DEPTH):
        z = rmsnorm(x, norm_mix_g[l])
        proj = z @ w_in[l]
        (ml_qk, ml_v, ml_o, ml_g, hg_q, hg_ff, hg_fb, hg_i, hg_g,
         gate_m, gate_h) = split_cols(proj, IN_SPLITS)

        qk = jax.nn.silu(dwconv(ml_qk, ml_conv_w[l], ml_conv_b[l]))
        q_m = to_heads(qk[..., :ML_DIM], ML_HEADS).astype(f32)
        k_m = to_heads(qk[..., ML_DIM:], ML_HEADS).astype(f32) * (ML_HEAD_DIM ** -0.5)
        v_m = to_heads(ml_v, ML_HEADS).astype(f32)
        gates = (ml_g.reshape(bsz, seq, 4, ML_HEADS) + ml_gate_b[l].astype(dt)).astype(f32)
        gates = gates.transpose(2, 0, 3, 1)
        h_fwd = mlstm_scan(q_m, k_m, v_m, gates[0], jax.nn.log_sigmoid(gates[1]))
        h_bwd = flip(mlstm_scan(flip(q_m), flip(k_m), flip(v_m), flip(gates[2]),
                                flip(jax.nn.log_sigmoid(gates[3]))))
        y_m = (head_rmsnorm(h_fwd + h_bwd, ml_norm_g[l]) * jax.nn.sigmoid(ml_o.astype(f32))).astype(dt)

        lb = lb_all[:, l].reshape(2, HG_HEADS, 1, HG_EXPAND)
        q_h = to_heads(jax.nn.silu(hg_q), HG_HEADS).astype(f32)
        v_h = to_heads(hg_i, HG_HEADS).astype(f32)
        f_fwd = lb[0] + (1.0 - lb[0]) * jax.nn.sigmoid(to_heads(hg_ff, HG_HEADS).astype(f32))
        f_bwd = lb[1] + (1.0 - lb[1]) * jax.nn.sigmoid(to_heads(hg_fb, HG_HEADS).astype(f32))
        o_fwd = hgrn2_scan(q_h, 1.0 - f_fwd, v_h, jnp.log(f_fwd))
        o_bwd = flip(hgrn2_scan(flip(q_h), flip(1.0 - f_bwd), flip(v_h), flip(jnp.log(f_bwd))))
        y_h = (head_rmsnorm(o_fwd + o_bwd, hg_norm_g[l]) * jax.nn.silu(hg_g.astype(f32))).astype(dt)

        merged = jax.nn.sigmoid(gate_m) * (y_m @ w_branch_m[l]) + jax.nn.sigmoid(gate_h) * (y_h @ w_branch_h[l])
        x = x + merged @ w_out[l]

        u = rmsnorm(x, norm_x_g[l])
        mn = rmsnorm(mem, norm_mem_g[l])
        q_x = (u @ w_q_x[l]).reshape(bsz, seq, X_HEADS, X_HEAD_DIM)
        kv = (mn @ w_kv_x[l]).reshape(bsz, N_MEM, 2, X_HEADS, X_HEAD_DIM)
        scores = jnp.einsum('bshd,bmhd->bhsm', q_x.astype(f32), kv[:, :, 0].astype(f32)) * (X_HEAD_DIM ** -0.5)
        probs = jax.nn.softmax(scores, axis=-1).astype(dt)
        att = jnp.einsum('bhsm,bmhd->bshd', probs, kv[:, :, 1]).reshape(bsz, seq, D_MODEL)
        x = x + att @ w_o_x[l]

        u = rmsnorm(x, norm_ffn_g[l])
        up = u @ w_up[l]
        a = dwconv(up[..., :D_FF], ffn_conv_w[l], ffn_conv_b[l])
        x = x + (jax.nn.gelu(a) * up[..., D_FF:]) @ w_down[l]

    return rmsnorm(x, norm_final_g)


_drawn_inputs = setup_inputs


def setup_inputs(seed=0):
    import zlib

    import numpy as np

    out = dict(_drawn_inputs(seed))
    spreads = {}
    factors = {'norm_mix_g': 3.933,
     'ml_conv_b': 64.0,
     'ml_norm_g': 21.671,
     'hg_lb': 8.0,
     'hg_norm_g': 8.0,
     'norm_x_g': 8.0,
     'norm_mem_g': 8.0,
     'norm_ffn_g': 14.424,
     'ffn_conv_b': 19.316,
     'norm_final_g': 8.441}
    for name, (base, spread) in spreads.items():
        noise = np.random.default_rng([zlib.crc32(name.encode()), seed]).standard_normal(out[name].shape)
        drawn = base * np.exp(spread * noise) if base else spread * noise
        out[name] = __import__('jax').numpy.asarray(drawn.astype(out[name].dtype))
    for name, factor in factors.items():
        out[name] = (out[name] * factor).astype(out[name].dtype)
    return out
```

```python
from contextlib import ExitStack

import concourse.bass as bass
from concourse import mybir

ALU = mybir.AluOpType
ACT = mybir.ActivationFunctionType
F32 = mybir.dt.float32
F32R = mybir.dt.float32r
U8 = mybir.dt.uint8
AX_X = mybir.AxisListType.X

P = 128
D = 1024
T = 1024
M = 256
KT = D // P
NT = T // P
HALF = T // 2
BC = 256
FF = 2816
EPS = 1e-6
ML_HEADS, HG_HEADS, X_HEADS = 4, 8, 4
LEVELS = 7
ROWS = 36
BWD = 32
GATE_COL = 4096
HG_T_COL, HG_N_COL, MERGE_COL = 4112, 7184, 9232


class Blk:

    def __init__(self, base, i=0, step=0):
        self.base, self.i, self.step = base, i, step
        self.slot = base % 2

    def ahead(self, k):
        return Blk(self.base + k, self.i, self.step)

    def count(self, k=0):
        return self.i * self.step + (self.base + 1 + k) if self.step else self.base + 1 + k

    def slot_dmas(self):
        c = 16 * (self.base // 2 + 1)
        return self.i * (8 * self.step) + c if self.step else c

    def unit(self, u, k=0):
        c = FIRST_UNITS + 4 * (self.base - k - KV - 1) + u + 1
        return self.i * (4 * self.step) + c if self.step else c


KV = 8
FIRST_UNITS = KV + 2
B_HGT = KV + 1
B_HGN = B_HGT + 12
B_ML = B_HGN + 8
B_GATE = B_ML + 16
B_BRANCH = B_GATE + 8
B_OUT = B_BRANCH + 8
B_Q = B_OUT + 4
B_O = B_Q + 4
B_FF = B_O + 4
NFF = FF // BC
B_END = B_FF + 3 * NFF


class Line:

    def __init__(self, eng, sem):
        self.eng, self.sem, self.n = eng, sem, 0

    def __call__(self, ins):
        self.n += 1
        ins.then_inc(self.sem, 1)
        self.eng.wait_ge(self.sem, self.n)

    def free(self, ins):
        self.n += 1
        ins.then_inc(self.sem, 1)

    def restart(self):
        self.eng.sem_clear(self.sem)
        self.n = 0


def signal(eng, ins, sem, value):
    ins.then_inc(sem, 1)
    eng.wait_ge(sem, value)


def view(t, off, *dims):
    a = t[:]
    return bass.AP(a.tensor, off, [list(a.ap[0])] + [list(d) for d in dims])


def at(i, n):
    return slice(i, i + n) if isinstance(i, int) else bass.ds(i, n)


def level_tot(l):
    return sum(2 * (T >> k) for k in range(1, l))


def build(nc, A, out, stop=99):
    x, mem = A["x"][0], A["mem"][0]
    w_in = A["w_in"][0].rearrange("(k p) n -> p k n", p=P)

    def wk(name):
        return A[name][0].rearrange("(k p) n -> p k n", p=P)

    with ExitStack() as ctx:
        def sb(name, shape, dt=F32, c=ctx):
            return c.enter_context(nc.sbuf_tensor(name, shape, dt))

        def sem(name):
            return ctx.enter_context(nc.semaphore(name))

        def dram(name, shape):
            return nc.dram_tensor(name, shape, F32, kind="Internal").ap()

        gT = dram("gate_rows", [16, T])
        rowsD = dram("decay_rows", [2, ROWS, T])
        hT = dram("hg_T", [3072, T])
        hN = dram("hg_N", [T, 2048])
        mT = dram("ml_T", [2048, T])
        mN = dram("ml_N", [T, 2048])
        mgT = dram("merge_gates_T", [2048, T])
        yT_d = dram("branch_T", [2048, T])
        mergedT = dram("merged_T", [D, T])
        x2_d = dram("x_after_mix", [T, D])
        x3_d = dram("x_after_attention", [T, D])
        attT_d = dram("attended_T", [D, T])
        kxT_d = dram("mem_keys_T", [D, M])
        vx_d = dram("mem_values", [M, D])

        ident = sb("ident", [P, P])
        lmask = sb("lmask", [P, LEVELS, P], U8)
        cmask = sb("cmask", [P, 2, P])
        ones = sb("ones", [P, P])
        onehot = sb("onehot", [ROWS, ML_HEADS])
        sel8 = sb("sel8", [ROWS, 8])
        dirsel = sb("dirsel", [ROWS, 2, P])
        gate_bias = sb("gate_bias", [ROWS, 2])
        lb = sb("lb", [P, 2, HG_HEADS])
        lb_rest = sb("lb_rest", [P, 2, HG_HEADS])
        lb_h = sb("lb_h", [P, 2, 2])
        colT = sb("colT", [P, 200])
        lb_raw = colT[:, 0:32].rearrange("p (d l h) -> p d l h", d=2, l=2)
        hg_g, ml_g, mcb = colT[:, 32:40], colT[:, 40:48], colT[:, 48:64]
        mcw = colT[:, 64:112].rearrange("p (w k) -> p w k", w=3)
        fcb = colT[:, 112:134]
        fcw = colT[:, 134:200].rearrange("p (w k) -> p w k", w=3)
        cw = sb("cw", [P, 2, 4])
        cols = sb("cols", [P, 3, NT, 2, ML_HEADS])
        decb = sb("decb", [P, NT, 2, ML_HEADS])
        hcol = sb("hcol", [P, 3, NT, 2])
        hdec = sb("hdec", [P, NT, 2])
        ss = sb("ss", [P, 2, 8])
        rstd = sb("rstd", [P, 2, 8])
        negh = sb("negh", [P, 1])
        per_ml = sb("per_ml", [P, 1])
        per_hg = sb("per_hg", [P, 1])
        eps_col = sb("eps_col", [P, 1])
        gcol = sb("gcol", [P, 2])
        raw = sb("raw", [P, 2, KT * BC])
        whi = sb("whi", [P, 2, KT, BC], F32R)
        wlo = sb("wlo", [P, 2, KT, BC], F32R)
        ev = sb("ev", [P, 4, HALF])
        w4 = raw[:, :, :].rearrange("p s (k n) -> p s k n", k=KT)

        nA = ExitStack()
        a_hi = sb("a_hi", [P, KT, T], F32R, nA)
        a_lo = sb("a_lo", [P, KT, T], F32R, nA)

        def norm_bufs(tag, c):
            return dict(xt=sb("xt" + tag, [P, 2, D], F32, c), xn=sb("xn" + tag, [P, 2, D], F32, c),
                        junk=sb("junk" + tag, [P, D], F32, c), gb=sb("gb" + tag, [P, D], F32, c))

        with ExitStack() as c:
            nb = norm_bufs("_0", c)
            gi = sb("gi", [ROWS, T], F32, c)
            gf = sb("gf", [ROWS, T], F32, c)
            gm = sb("gm", [ROWS, T], F32, c)
            gbc = sb("gbc", [ROWS, T], F32, c)
            gw = sb("gw", [ROWS, 3, T], F32, c)
            greset = sb("greset", [ROWS, T], F32, c)
            gms = sb("gms", [ROWS, NT], F32, c)
            gre = sb("gre", [ROWS, NT], F32, c)
            prow = sb("prow", [P, 2, P], F32, c)
            gdec = sb("gdec", [ROWS, NT], F32, c)
            gds = sb("gds", [ROWS, NT, 8], F32, c)
            lmask_f = sb("lmask_f", [P, LEVELS, P], F32, c)
        with ExitStack() as c:
            qfb = sb("qfb", [P, 3, T], F32, c)
            vg = sb("vg", [P, 2, NT, P], F32, c)
            fkd = sb("fkd", [P, 2, T], F32, c)
            tot = sb("tot", [P, 2 * (T - NT)], F32, c)
            X = sb("X", [P, 2, T], F32, c)
            Y = sb("Y", [P, 2, T], F32, c)
            Yc = sb("Yc", [P, T], F32, c)
            qs = sb("qs", [P, T], F32, c)
            Am = sb("Am", [P, NT, P], F32, c)
            Sall = sb("Sall", [P, 2, NT, P], F32, c)
            cv = sb("cv", [P, T], F32, c)
            cs = sb("cs", [P, T], F32, c)
            gv = cs[:].rearrange("p (c v) -> p c v", c=NT)
        with ExitStack() as c:
            rows = sb("rows", [ROWS, 2, T], F32, c)
            rsel = sb("rsel", [ROWS, 2, T], F32, c)
            mq = sb("mq", [P, 2, T], F32, c)
            mk = sb("mk", [P, 2, T], F32, c)
            mv = sb("mv", [P, NT, BC], F32, c)
            mo = sb("mo", [P, NT, BC], F32, c)
            kN = sb("kN", [P, NT, BC], F32, c)
            Hm = sb("Hm", [P, NT, BC], F32, c)
            C = sb("C", [P, 2, 2, BC + 1], F32, c)
            Dm = sb("Dm", [P, 2, P], F32, c)
            Em = sb("Em", [P, 2, P], F32, c)
            Pm = sb("Pm", [P, 2, P], F32, c)
            kw = sb("kw", [P, 2, BC], F32, c)
            inter = sb("inter", [P, 2, BC], F32, c)
            num = sb("num", [P, 2, BC], F32, c)
            den = sb("den", [P, 4, 2], F32, c)
            sq = sb("sq", [P, 2, BC], F32, c)
        with ExitStack() as c:
            b_hi = sb("b_hi", [P, KT, T], F32R, c)
            b_lo = sb("b_lo", [P, KT, T], F32R, c)
            mg = sb("mg", [P, 2, T], F32, c)
            gt = sb("gt", [P, 2, T], F32, c)
        nA.close()
        with ExitStack() as c:
            na = norm_bufs("_A", c)
        with ExitStack() as c:
            kx = sb("kx", [P, 8, M], F32, c)
            vx = sb("vx", [P, 2, D], F32, c)
            PT = sb("PT", [P, 2, T], F32, c)
            pr = sb("pr", [P, 2, M], F32, c)
            atS = sb("atS", [P, 2, T], F32, c)
            mx = sb("mx", [P, 2, 3], F32, c)
        with ExitStack() as c:
            acc = sb("acc", [P, NT, D], F32, c)
            ga = sb("ga", [P, 2, T], F32, c)
            h_hi = sb("h_hi", [P, 2, T], F32R, c)
            h_lo = sb("h_lo", [P, 2, T], F32R, c)
        ps = ctx.enter_context(nc.psum_tensor("ps", [P, 8, 512], F32))
        psw = ps[:, :, :].rearrange("p b n -> p (b n)")

        const_ld, param_ld, g2_ld, nld2_0, nld2_1, ones_done, col_tr, col_ready = [
            sem(n) for n in ("const_ld", "param_ld", "g2_ld", "nld2_0", "nld2_1", "ones_done", "col_tr", "col_ready")]
        col_done, w_ld0, w_ld1, w_hi, w_lo, unit_done, ev_done, st0 = [
            sem(n) for n in ("col_done", "w_ld0", "w_ld1", "w_hi", "w_lo", "unit_done", "ev_done", "st0")]
        st1, kv_st0, kv_st1, nld0, nld1, g_ld, n_sq, n_rs = [
            sem(n) for n in ("st1", "kv_st0", "kv_st1", "nld0", "nld1", "g_ld", "n_sq", "n_rs")]
        n_mul, n_tr, n_hi, n_lo, grow_zero, grow_ld, grow_dve, grow_act = [
            sem(n) for n in ("n_mul", "n_tr", "n_hi", "n_lo", "grow_zero", "grow_ld", "grow_dve", "grow_act")]
        g_tr, rows_st, act_line, dve_line, pool_line, h_qld, h_vld, h_sig = [
            sem(n) for n in ("g_tr", "rows_st", "act_line", "dve_line", "pool_line", "h_qld", "h_vld", "h_sig")]
        h_init, h_lv, h_upd, h_updy, h_yc, h_pred, h_diag, h_kdt = [
            sem(n) for n in ("h_init", "h_lv", "h_upd", "h_updy", "h_yc", "h_pred", "h_diag", "h_kdt")]
        h_kd, h_u, h_s, h_o, h_ss, h_sq, h_rs, h_gate = [
            sem(n) for n in ("h_kd", "h_u", "h_s", "h_o", "h_ss", "h_sq", "h_rs", "h_gate")]
        h_silu, h_y, h_yt, h_ytc, h_st, conv_rd, conv_sig, conv_st = [
            sem(n) for n in ("h_silu", "h_y", "h_yt", "h_ytc", "h_st", "conv_rd", "conv_sig", "conv_st")]
        m_ld, m_rows_ld, m_kt, m_kn, m_sel, m_sc, m_arg, m_exp = [
            sem(n) for n in ("m_ld", "m_rows_ld", "m_kt", "m_kn", "m_sel", "m_sc", "m_arg", "m_exp")]
        m_p, m_kw, m_int, m_icp, m_upf, m_cf, m_in, m_hm = [
            sem(n) for n in ("m_p", "m_kw", "m_int", "m_icp", "m_upf", "m_cf", "m_in", "m_hm")]
        m_upb, m_cb, m_sq, m_ss, m_rs, m_og, m_yn, m_y = [
            sem(n) for n in ("m_upb", "m_cb", "m_sq", "m_ss", "m_rs", "m_og", "m_yn", "m_y")]
        m_yt, m_ytc, m_st, op_ld0, op_ld1, op_hi, op_lo, gt_ld0 = [
            sem(n) for n in ("m_yt", "m_ytc", "m_st", "op_ld0", "op_ld1", "op_hi", "op_lo", "gt_ld0")]
        gt_ld1, gt_sig, br_done, br_st0, br_st1, res_ld0, res_ld1, res_done = [
            sem(n) for n in ("gt_ld1", "gt_sig", "br_done", "br_st0", "br_st1", "res_ld0", "res_ld1", "res_done")]
        res_st0, res_st1, kx_ld, a_sc, a_mx, a_exp, a_nrm, a_tr = [
            sem(n) for n in ("res_st0", "res_st1", "kx_ld", "a_sc", "a_mx", "a_exp", "a_nrm", "a_tr")]
        a_pt, a_att, a_ev, a_st, acc_ld, f_conv, f_gelu, f_mul = [
            sem(n) for n in ("a_pt", "a_att", "a_ev", "a_st", "acc_ld", "f_conv", "f_gelu", "f_mul")]
        f_hi, f_lo, f_dn, f_acc, fin_sq, fin_rs, fin_mul, fin_st = [
            sem(n) for n in ("f_hi", "f_lo", "f_dn", "f_acc", "fin_sq", "fin_rs", "fin_mul", "fin_st")]
        h_sgate, h_q, h_keys, h_ksum = [sem(n) for n in ("h_sgate", "h_q", "h_keys", "h_ksum")]
        m_qk_ld, m_v_ld, m_o_ld = [sem(n) for n in ("m_qk_ld", "m_v_ld", "m_o_ld")]
        w_ld, st, kv_st, nld = (w_ld0, w_ld1), (st0, st1), (kv_st0, kv_st1), (nld0, nld1)
        nld2 = (nld2_0, nld2_1)
        op_ld, gt_ld, br_st = (op_ld0, op_ld1), (gt_ld0, gt_ld1), (br_st0, br_st1)
        res_ld, res_st = (res_ld0, res_ld1), (res_st0, res_st1)

        block = ctx.enter_context(nc.Block())
        NORM0 = [("mem", t) for t in range(2)] + [("x", t) for t in (2, 3, 4, 5, 6, 7, 0, 1)]
        NORM1 = [("x2", t) for t in range(NT)]
        NORM2 = [("x3", t) for t in range(NT)]
        FORDER = ff_order()


        @block.sync
        def _(sp):
            for t, name in ((ident, "c_ident"), (lmask_f, "c_lmask"), (cmask, "c_cmask"), (onehot, "c_onehot"),
                            (sel8, "c_sel8"), (dirsel, "c_dirsel"), (greset, "c_reset")):
                sp.dma_start(t[:], A[name]).then_inc(const_ld, 16)

            def weights(b, src):
                if b.step or b.base >= 2:
                    sp.wait_ge(w_lo, b.count(-2))
                sp.dma_start(w4[:, b.slot], src).then_inc(w_ld[b.slot], 16)

            def stream(base, count, col):
                with sp.Fori(0, count // 2) as i:
                    for j in range(2):
                        c = sp.snap(i * (2 * BC) + (col + j * BC))
                        weights(Blk(base + j, i, 2), w_in[:, :, at(c, BC)])

            w_kv = wk("w_kv_x")
            for w, (name, t) in enumerate(NORM0):
                if w == 0:
                    sp.dma_start(nb["gb"][:], A["norm_mem_g"].to_broadcast([P, D])).then_inc(g_ld, 16)
                if w == 2:
                    sp.wait_ge(n_mul, 2)
                    sp.dma_start(nb["gb"][:], A["norm_mix_g"].to_broadcast([P, D])).then_inc(g_ld, 16)
                if w >= 2:
                    sp.wait_ge(n_mul, w - 1)
                src = mem if name == "mem" else x
                sp.dma_start(nb["xt"][:, w % 2], src[t * P:(t + 1) * P, :]).then_inc(nld[w % 2], 16)
                if w >= 1 and w - 1 < KV:
                    weights(Blk(w - 1), w_kv[:, :, (w - 1) * BC:w * BC])
            weights(Blk(KV), w_in[:, :, GATE_COL:GATE_COL + BC])
            stream(B_HGT, 12, HG_T_COL)
            stream(B_HGN, 8, HG_N_COL)
            with sp.Fori(0, 8) as i:
                for j, col in ((0, 0), (1, 2048)):
                    c = sp.snap(i * BC + col)
                    weights(Blk(B_ML + j, i, 2), w_in[:, :, at(c, BC)])
            if stop <= 2:
                weights(Blk(B_GATE), w_in[:, :, MERGE_COL:MERGE_COL + BC])
                return
            stream(B_GATE, 8, MERGE_COL)
            if stop <= 3:
                weights(Blk(B_BRANCH), wk("w_branch_h")[:, :, 0:BC])
                return
            wbh, wbm = wk("w_branch_h"), wk("w_branch_m")
            for j in range(4):
                weights(Blk(B_BRANCH + 2 * j), wbh[:, :, j * BC:(j + 1) * BC])
                weights(Blk(B_BRANCH + 2 * j + 1), wbm[:, :, j * BC:(j + 1) * BC])
            for b0, name in ((B_OUT, "w_out"), (B_Q, "w_q_x"), (B_O, "w_o_x")):
                for j in range(4):
                    weights(Blk(b0 + j), wk(name)[:, :, j * BC:(j + 1) * BC])
            wup = wk("w_up")
            wdn = A["w_down"][0].rearrange("(g k p) n -> g p k n", k=2, p=P)
            raw_dn = raw[:, :, :].rearrange("p s (k n) -> p s k n", k=2)
            for n, (kind, g) in enumerate(FORDER):
                b = Blk(B_FF + n)
                if kind == "down":
                    sp.wait_ge(w_lo, b.count(-2))
                    sp.dma_start(raw_dn[:, b.slot], wdn[g]).then_inc(w_ld[b.slot], 16)
                else:
                    c = (FF if kind == "b" else 0) + g * BC
                    weights(b, wup[:, :, c:c + BC])

        @block.gpsimd
        def _(pool):
            line = Line(pool, pool_line)
            for t in (gi, gf, gm, gbc, gms, gre):
                line.free(pool.memset(t[:], 0.0))
            line(pool.memset(ones[:], 1.0))
            line(pool.memset(per_ml[:], 1.0 / BC))
            line(pool.memset(per_hg[:], 1.0 / P))
            line(pool.memset(eps_col[:], EPS))
            signal(pool, pool.memset(negh[:], -0.5), ones_done, 1)
            r = 0
            for src in (A["hg_lb"].rearrange("d l (h p) -> (d l h) p", p=P), A["hg_norm_g"].rearrange("a (k p) -> (a k) p", p=P),
                        A["ml_norm_g"].rearrange("a (k p) -> (a k) p", p=P), A["ml_conv_b"].rearrange("a (k p) -> (a k) p", p=P),
                        A["ml_conv_w"][0].rearrange("w (k p) -> (w k) p", p=P), A["ffn_conv_b"].rearrange("a (k p) -> (a k) p", p=P),
                        A["ffn_conv_w"][0].rearrange("w (k p) -> (w k) p", p=P)):
                n = src.shape[0]
                pool.dma_start(prow[r % 112:r % 112 + n, r // 112], src).then_inc(param_ld, 16)
                r += n
            gbias = A["ml_gate_b"][0].rearrange("g h -> h g")
            for d in range(2):
                pool.dma_start(gate_bias[BWD * d:BWD * d + 4, :], gbias[:, 2 * d:2 * d + 2],
                               allow_slow_non_contiguous=True).then_inc(param_ld, 16)

            def norm_rs(w):
                pool.wait_ge(n_sq, w + 1)
                line(pool.tensor_scalar(rstd[:, 0, w % 2:w % 2 + 1], ss[:, 0, w % 2:w % 2 + 1], 1.0 / D, EPS, ALU.mult, ALU.add))
                signal(pool, pool.tensor_tensor(rstd[:, 0, w % 2:w % 2 + 1], rstd[:, 0, w % 2:w % 2 + 1], negh[:], ALU.pow), n_rs, w + 1)

            for w in range(len(NORM0)):
                if w >= 2:
                    pool.wait_ge(n_mul, w - 1)
                norm_rs(w)
            pool.wait_ge(st[0], 16)
            for d in range(2):
                pool.dma_start(gi[BWD * d:BWD * d + 4], gT[8 * d:8 * d + 4, :]).then_inc(grow_ld, 16)
                pool.dma_start(gf[BWD * d:BWD * d + 4], gT[8 * d + 4:8 * d + 8, :]).then_inc(grow_ld, 16)
            pool.wait_ge(grow_dve, 2)
            pool.dma_start(rowsD[0], gbc[:]).then_inc(rows_st, 16)
            pool.dma_start(rowsD[1], gi[:]).then_inc(rows_st, 16)
            pool.wait_ge(st[0], 16 * 21)
            pool.wait_ge(st[1], 16 * 20)
            pool.wait_ge(rows_st, 32)
            pool.wait_ge(grow_act, 4)
            pool.wait_ge(g_tr, 1)

            def load_q(h):
                for k in range(3):
                    r = h * P + k * D if isinstance(h, int) else pool.snap(h * P + k * D)
                    pool.dma_start(qfb[:, k], hT[at(r, P), :]).then_inc(h_qld, 16)

            def load_v(h):
                for k in range(2):
                    c = h * P + k * D if isinstance(h, int) else pool.snap(h * P + k * D)
                    pool.dma_start(vg[:, k], hN[:, at(c, P)].rearrange("(c p) n -> p c n", p=P)).then_inc(h_vld, 16)

            def hg_pool(h, last):
                line.restart()
                if not last:
                    pool.wait_ge(h_init, h + 1)
                    load_q(h + 1)
                for c in range(2):
                    pool.wait_ge(conv_sig, h * 2 + c + 1)
                    line(pool.tensor_tensor(cv[:], cv[:], cs[:], ALU.mult))
                    r = h * BC + c * P if isinstance(h, int) else pool.snap(h * BC + c * P)
                    pool.dma_start(mT[at(r, P), :], cv[:]).then_inc(conv_st, 16)
                pool.wait_ge(h_gate, h + 1)
                signal(pool, pool.tensor_tensor(gv, gv, vg[:, 1], ALU.mult), h_silu, h + 1)
                pool.wait_ge(h_ss, h + 1)
                line(pool.tensor_tensor(rstd[:, 1], ss[:, 1], per_hg[:].to_broadcast([P, 8]), ALU.mult))
                line(pool.tensor_tensor(rstd[:, 1], rstd[:, 1], eps_col[:].to_broadcast([P, 8]), ALU.add))
                signal(pool, pool.tensor_tensor(rstd[:, 1], rstd[:, 1], negh[:].to_broadcast([P, 8]), ALU.pow), h_rs, h + 1)
                if not last:
                    pool.wait_ge(h_o, h + 1)
                    load_v(h + 1)

            load_q(0)
            load_v(0)
            hg_pool(0, False)
            with pool.Fori(1, HG_HEADS - 1) as h:
                hg_pool(h, False)
            hg_pool(HG_HEADS - 1, True)
            if stop <= 2:
                pool.wait_ge(conv_st, 256)
                return

            pool.wait_ge(conv_st, 256)
            pool.wait_ge(st[0], 16 * 29)
            pool.wait_ge(st[1], 16 * 28)
            pool.wait_ge(h_st, 128)
            pool.dma_start(rows[:, 0], rowsD[0]).then_inc(m_rows_ld, 16)
            pool.dma_start(rows[:, 1], rowsD[1]).then_inc(m_rows_ld, 16)

            def ml_cols(j, k):
                return at(j * BC + k * D if isinstance(j, int) else pool.snap(j * BC + k * D), BC)

            def load_qk(j):
                for k, t in enumerate((mq, mk)):
                    pool.dma_start(t[:], mT[ml_cols(j, k), :].rearrange("(k p) t -> p k t", p=P)).then_inc(m_qk_ld, 16)

            def load_mv(j):
                pool.dma_start(mv[:], mN[:, ml_cols(j, 0)].rearrange("(c p) n -> p c n", p=P)).then_inc(m_v_ld, 16)

            def ml_pool(j, first, last=False):
                line.restart()
                pool.wait_ge(m_kn, j + 1)
                pool.wait_ge(m_sel, j + 1)
                for s in range(NT):
                    if s:
                        pool.wait_ge(m_upb, j * NT + s)
                    jump = NT - 1 - 2 * s
                    pool.tensor_tensor(kw[:], view(kN, s * BC, [jump * BC, 2], [1, BC]),
                                       view(hcol, 4 * NT + 2 * s, [2 * jump + 1, 2], [0, BC]), ALU.mult).then_inc(m_kw, 1)
                    if s == 0:
                        if not first:
                            pool.wait_ge(m_st, j * 16)
                        pool.dma_start(mo[:], mN[:, ml_cols(j, 1)].rearrange("(c p) n -> p c n", p=P)).then_inc(m_o_ld, 16)
                if not last:
                    pool.wait_ge(m_int, j * NT + NT)
                    load_qk(j + 1)
                    pool.wait_ge(m_upb, j * NT + NT)
                    load_mv(j + 1)
                pool.wait_ge(m_ss, j + 1)
                line(pool.tensor_tensor(rstd[:, 1], ss[:, 1], per_ml[:].to_broadcast([P, 8]), ALU.mult))
                line(pool.tensor_tensor(rstd[:, 1], rstd[:, 1], eps_col[:].to_broadcast([P, 8]), ALU.add))
                signal(pool, pool.tensor_tensor(rstd[:, 1], rstd[:, 1], negh[:].to_broadcast([P, 8]), ALU.pow), m_rs, j + 1)

            load_qk(0)
            load_mv(0)
            ml_pool(0, True)
            with pool.Fori(1, ML_HEADS - 1) as j:
                ml_pool(j, False)
            ml_pool(ML_HEADS - 1, False, True)
            if stop <= 3:
                return

            pool.wait_ge(m_st, 64)

            def operand_loads(o0, src):
                for k in range(KT):
                    o = o0 + k
                    if o >= 2:
                        pool.wait_ge(op_lo, o - 1)
                    pool.dma_start(gt[:, o % 2], src[k * P:(k + 1) * P, :]).then_inc(op_ld[o % 2], 16)
            operand_loads(0, yT_d[D:2 * D, :])
            operand_loads(KT, yT_d[0:D, :])
            pool.wait_ge(op_lo, 2 * KT)
            pool.wait_ge(st[0], 16 * 37)
            pool.wait_ge(st[1], 16 * 36)
            q = 0
            for j in range(4):
                for kind in (1, 0):
                    for c in range(2):
                        if q >= 2:
                            pool.wait_ge(br_done, q - 1)
                        r = kind * D + j * BC + c * P
                        pool.dma_start(gt[:, q % 2], mgT[r:r + P, :]).then_inc(gt_ld[q % 2], 16)
                        q += 1

            def residuals(q0, src, free):
                for q in range(q0, q0 + 8):
                    j, c = (q - q0) // 2, q % 2
                    if q < q0 + 2:
                        free(c)
                    else:
                        pool.wait_ge(res_st[c], 16 * (q // 2))
                    pool.dma_start(mg[:, c].rearrange("p (j n) -> p j n", n=BC),
                                   src[c * 512:(c + 1) * 512, j * BC:(j + 1) * BC].rearrange("(j p) n -> p j n", p=P)) \
                        .then_inc(res_ld[c], 16)

            for c in range(2):
                pool.wait_ge(br_st[c], 64)
            operand_loads(2 * KT, mergedT)
            residuals(0, x, lambda c: None)

            def norm_loads(tiles, w0, src, gain):
                pool.dma_start(na["gb"][:], gain.to_broadcast([P, D])).then_inc(g2_ld, 16)
                for k, (_, t) in enumerate(tiles):
                    w = w0 + k
                    if k >= 2:
                        pool.wait_ge(n_mul, w - 1)
                    pool.dma_start(na["xt"][:, w % 2], src[t * P:(t + 1) * P, :]).then_inc(nld2[w % 2], 16)
                    if k >= 1:
                        norm_rs(w - 1)
                norm_rs(w0 + len(tiles) - 1)
            for c in range(2):
                pool.wait_ge(res_st[c], 64)
            norm_loads(NORM1, 10, x2_d, A["norm_x_g"])
            pool.wait_ge(n_lo, 18)
            pool.dma_start(kx[:], kxT_d.rearrange("(k p) m -> p k m", p=P)).then_inc(kx_ld, 16)
            pool.dma_start(vx[:], vx_d.rearrange("(c p) n -> p c n", p=P)).then_inc(kx_ld, 16)
            pool.wait_ge(a_st, 64)
            operand_loads(3 * KT, attT_d)
            residuals(8, x2_d, lambda c: None)
            for c in range(2):
                pool.wait_ge(res_st[c], 128)
            norm_loads(NORM2, 18, x3_d, A["norm_ffn_g"])
            pool.wait_ge(n_lo, 26)
            pool.dma_start(acc[:], x3_d.rearrange("(t p) n -> p t n", p=P)).then_inc(acc_ld, 16)
            pool.dma_start(mg[:, 0], A["norm_final_g"].rearrange("(a n) -> a n", a=1).to_broadcast([P, D])).then_inc(acc_ld, 16)
            for t in range(NT):
                pool.wait_ge(fin_sq, t + 1)
                line(pool.tensor_scalar(rstd[:, 1, t:t + 1], ss[:, 1, t:t + 1], 1.0 / D, EPS, ALU.mult, ALU.add))
                signal(pool, pool.tensor_tensor(rstd[:, 1, t:t + 1], rstd[:, 1, t:t + 1], negh[:], ALU.pow), fin_rs, t + 1)

        @block.scalar
        def _(act):
            line = Line(act, act_line)

            def split_hi(b):
                act.wait_ge(w_ld[b.slot], b.slot_dmas())
                if b.step or b.base >= 2:
                    wait_used(act, b.ahead(-2))
                signal(act, act.activation(whi[:, b.slot], w4[:, b.slot], ACT.Copy), w_hi, b.count())

            def wait_used(eng, b):
                if not b.step and b.base >= B_FF:
                    n = b.base - B_FF
                    kind, g = FORDER[n]
                    if kind == "down":
                        eng.wait_ge(f_dn, 16 * (g + 1))
                    else:
                        eng.wait_ge(unit_done, ff_unit(kind, g, 3))
                elif b.step or b.base > KV:
                    eng.wait_ge(unit_done, b.unit(3))
                else:
                    eng.wait_ge(unit_done, FIRST_UNITS if b.base == KV else b.base + 1)

            def unit_out(b, u):
                act.wait_ge(unit_done, b.unit(u))
                signal(act, act.activation(ev[:, u], ps[:, u], ACT.Copy), ev_done, b.unit(u))

            def norm_sq(w, bufs):
                if w < 10:
                    act.wait_ge(nld[w % 2], 16 * (w // 2 + 1))
                else:
                    act.wait_ge(nld2[w % 2], 16 * (w // 2 - 4))
                if w >= 2:
                    act.wait_ge(n_rs, w - 1)
                signal(act, act.activation(bufs["junk"][:], bufs["xt"][:, w % 2], ACT.Square,
                                           accum_out=ss[:, 0, w % 2:w % 2 + 1]), n_sq, w + 1)

            def norm_hi(w, t, hi):
                act.wait_ge(n_tr, w + 1)
                b0 = (4 + 2 * (w % 2)) * 512
                signal(act, act.activation(hi[:, :, t * P:(t + 1) * P],
                                           psw[:, b0:b0 + D].rearrange("p (k t) -> p k t", k=KT), ACT.Copy), n_hi, w + 1)

            def kv_out(n):
                act.wait_ge(unit_done, n + 1)
                if n >= 2:
                    act.wait_ge(kv_st[n % 2], 16 * (n // 2))
                signal(act, act.activation(ev[:, n % 2], ps[:, n % 2], ACT.Copy), ev_done, n + 1)
                dst = kxT_d[n * BC:(n + 1) * BC, :] if n < 4 else vx_d[:, (n - 4) * BC:(n - 3) * BC]
                act.dma_start(dst.rearrange("(c p) m -> p c m", p=P),
                              ev[:, n % 2].rearrange("p (c m) -> p c m", c=2)).then_inc(kv_st[n % 2], 16)

            act.wait_ge(col_tr, 1)
            line.free(act.activation(colT[:, 0:112], ps[:, 0, 0:112], ACT.Copy))
            signal(act, act.activation(colT[:, 112:200], ps[:, 0, P:P + 88], ACT.Copy), col_ready, 1)
            norm_sq(0, nb)
            for w, (name, t) in enumerate(NORM0):
                if w + 1 < len(NORM0):
                    norm_sq(w + 1, nb)
                if w == 2:
                    split_hi(Blk(0))
                    split_hi(Blk(1))
                if w >= 2:
                    kv_out(w - 2)
                    split_hi(Blk(w))
                if w == 8:
                    act.wait_ge(unit_done, KV)
                norm_hi(w, t, a_hi)
            for u in range(2):
                act.wait_ge(unit_done, KV + 1 + u)
                act.wait_ge(kv_st[u], 64)
                signal(act, act.activation(ev[0:16, u], ps[0:16, u], ACT.Copy), ev_done, KV + 1 + u)
            act.dma_start(gT.rearrange("g (u n) -> g u n", u=2), ev[0:16, 0:2]).then_inc(st[0], 16)

            def raw_block(b, dst, stores, nxt=True):
                split_hi(b.ahead(1))
                for c in range(2):
                    if stores[c] is not None:
                        act.wait_ge(st[c], stores[c])
                    for u in (2 * c, 2 * c + 1):
                        unit_out(b, u)
                    dst(c)

            def put_t(t, row):
                def go(c):
                    r = row + c * P if isinstance(row, int) else row[c]
                    act.dma_start(t[at(r, P), :].rearrange("p (u n) -> p u n", u=2), ev[:, 2 * c:2 * c + 2]).then_inc(st[c], 16)
                return go

            def put_n(t, col):
                def go(c):
                    act.dma_start(t[c * 512:(c + 1) * 512, at(col, BC)].rearrange("(j p) n -> p j n", p=P),
                                  ev[:, 2 * c:2 * c + 2].rearrange("p u (j n) -> p (u j) n", n=BC)).then_inc(st[c], 16)
                return go

            act.wait_ge(col_done, 1)
            line(act.activation(lb[:], lb_raw[:, :, 1], ACT.Sigmoid))
            line(act.activation(lb_rest[:], lb_raw[:, :, 1], ACT.Sigmoid, scale=-1.0))
            for k in range(4):
                if k == 1:
                    act.wait_ge(grow_dve, 1)
                    line(act.activation(gw[:, 1], gw[:, 0], ACT.Exp))
                    signal(act, act.activation(gw[:, 1], gw[:, 1], ACT.Ln, bias=1.0), grow_act, 1)
                if k == 2:
                    act.wait_ge(grow_dve, 2)
                    line(act.activation(gw[:], gw[:], ACT.Exp))
                    signal(act, act.activation(gdec[:], gdec[:], ACT.Exp), grow_act, 2)
                raw_block(Blk(B_HGT + k), put_t(hT, k * BC), (16 * (k + 1), 16 * k if k else None))
            act.wait_ge(g_tr, 1)
            qc = cols[:].rearrange("p q c d h -> p (q c) d h")
            for b in range(2):
                ins = act.activation(qc[:, 12 * b:12 * b + 12],
                                     view(ps, (4 + b) * 512, [ROWS, 12], [BWD, 2], [1, 4]), ACT.Copy)
                line.free(ins)
            line(act.activation(decb[:].rearrange("p c d h -> p (c d h)"), ps[:, 6, 0:64], ACT.Copy))
            act.sem_inc(grow_act, 2)
            with act.Fori(2, 6) as i:
                for j in range(2):
                    row = [act.snap(i * (2 * BC) + (j * BC + c * P)) for c in range(2)]
                    raw_block(Blk(B_HGT + j, i, 2), put_t(hT, row), (i * 32 + (16 + 16 * j), i * 32 + 16 * j))
            with act.Fori(0, 4) as i:
                for j in range(2):
                    col = act.snap(i * (2 * BC) + j * BC)
                    raw_block(Blk(B_HGN + j, i, 2), put_n(hN, col), (i * 32 + 16 * (13 + j), i * 32 + 16 * (12 + j)))

            def next_gates(h):
                act.wait_ge(h_qld, h * 48 + 48)
                signal(act, act.activation(qfb[:, 1:3], qfb[:, 1:3], ACT.Sigmoid), h_sgate, h + 1)

            def next_queries(h):
                signal(act, act.activation(qs[:], qfb[:, 0], ACT.Sigmoid), h_sig, h + 1)

            def hg_act(h, step, last=False):
                line.restart()
                bT, bN = Blk(B_ML, h, step), Blk(B_ML + 1, h, step)
                col = act.snap(h * BC) if step else 0
                row = act.snap(h * P + D) if step else D
                split_hi(bN)

                def level_keys(l):
                    if l == 0:
                        act.wait_ge(h_keys, h + 1)
                        if step:
                            act.wait_ge(h_st, h * 16)
                    else:
                        act.wait_ge(h_updy, h * LEVELS + l)
                        act.wait_ge(h_lv, h * 8 + l + 1)
                    hh = 1 << l
                    signal(act, act.activation(view(Yc, 0, [2 * hh, (T >> l) // 2], [hh, 2], [1, hh]),
                                               view(Y, 0, [2 * hh, (T >> l) // 2], [T + hh, 2], [1, hh]), ACT.Copy),
                           h_yc, h * LEVELS + l + 1)

                def conv_sigmoid(c):
                    act.wait_ge(conv_rd, h * 2 + 1 + c)
                    if c or step:
                        act.wait_ge(conv_st, h * 32 + 16 * c)
                    signal(act, act.activation(cs[:], cv[:], ACT.Sigmoid), conv_sig, h * 2 + 1 + c)

                level_keys(0)
                act.wait_ge(h_lv, h * 8 + 1)
                if step:
                    act.wait_ge(h_o, h)
                signal(act, act.activation(Am[:], psw[:, 2048:3072].rearrange("p (c t) -> p c t", c=NT), ACT.Copy),
                       h_diag, h + 1)
                for l in range(1, LEVELS):
                    level_keys(l)
                    if l in (1, 3, 5):
                        u = l // 2
                        if u != 1:
                            act.wait_ge(st[u // 2], h * 16 + 16 * (21 - u // 2))
                        unit_out(bT, u)
                conv_sigmoid(0)
                for d in range(2):
                    act.wait_ge(h_kdt, h * 2 + 1 + d)
                    signal(act, act.activation(fkd[:, d], psw[:, 2048 + d * D:2048 + (d + 1) * D], ACT.Copy),
                           h_kd, h * 2 + 1 + d)
                    if d == 0:
                        unit_out(bT, 3)
                conv_sigmoid(1)
                split_hi(bN.ahead(1))
                if not last:
                    next_gates(h + 1)
                act.wait_ge(h_vld, h * 32 + 32)
                act.wait_ge(conv_st, h * 32 + 32)
                signal(act, act.activation(gv, vg[:, 1], ACT.Sigmoid), h_gate, h + 1)
                put = put_n(mN, col)
                unit_out(bN, 0)
                unit_out(bN, 1)
                put(0)
                act.wait_ge(h_o, h + 1)
                signal(act, act.activation(Sall[:, 0].rearrange("p c v -> p (c v)"), psw[:, 2048:3072], ACT.Square),
                       h_sq, h + 1)
                unit_out(bN, 2)
                act.wait_ge(h_yt, h + 1)
                if not last:
                    next_queries(h + 1)
                signal(act, act.activation(Yc[:], psw[:, 3072:4096], ACT.Copy, scale=gcol[:, 0:1]), h_ytc, h + 1)
                act.dma_start(yT_d[at(row, P), :], Yc[:]).then_inc(h_st, 16)
                unit_out(bN, 3)
                put(1)

            next_gates(0)
            next_queries(0)
            hg_act(0, 0)
            with act.Fori(1, HG_HEADS - 1) as h:
                hg_act(h, 2)
            hg_act(HG_HEADS - 1, 2, True)
            if stop <= 2:
                act.wait_ge(h_st, 128)
                act.wait_ge(st[0], 16 * 29)
                act.wait_ge(st[1], 16 * 28)
                return

            def ml_act(j, step):
                line.restart()
                b = [Blk(B_GATE, j, step), Blk(B_GATE + 1, j, step)]
                rowg = [[act.snap(j * (2 * BC) + k * BC + c * P) if step else k * BC + c * P for c in range(2)] for k in range(2)]
                rowy = act.snap(j * BC) if step else 0

                def gate_unit(k):
                    blk, u = b[k // 4], k % 4
                    c = u // 2
                    if u % 2 == 0:
                        act.wait_ge(st[c], j * 32 + 16 * (29 - c + k // 4))
                    unit_out(blk, u)
                    if u % 2:
                        act.dma_start(mgT[at(rowg[k // 4][c], P), :].rearrange("p (u n) -> p u n", u=2),
                                      ev[:, 2 * c:2 * c + 2]).then_inc(st[c], 16)

                def squares(s):
                    act.wait_ge(m_hm, j * NT + s + 1)
                    for d, c in ((0, s), (1, NT - 1 - s)):
                        ins = act.activation(sq[:, d], Hm[:, c], ACT.Square, accum_out=ss[:, 1, c:c + 1])
                        if d and s == NT - 1:
                            signal(act, ins, m_ss, j + 1)
                        elif d:
                            line(ins)
                        else:
                            line.free(ins)

                act.wait_ge(m_kt, j + 1)
                signal(act, act.activation(kN[:].rearrange("p c k -> p (c k)"), psw[:, 2048:4096], ACT.Copy,
                                           scale=BC ** -0.5), m_kn, j + 1)
                act.wait_ge(m_sel, j + 1)
                for s in range(NT):
                    g = j * NT + s
                    act.wait_ge(m_arg, g + 1)
                    if s:
                        act.wait_ge(m_p, g)
                    signal(act, act.activation(Em[:], Dm[:], ACT.Exp), m_exp, g + 1)
                    act.wait_ge(m_int, g + 1)
                    if s:
                        act.wait_ge(m_hm, g)
                    for d, c in ((0, s), (1, NT - 1 - s)):
                        ins = act.activation(inter[:, d], ps[:, 5, d * BC:(d + 1) * BC], ACT.Copy, scale=hcol[:, 0, c, d:d + 1])
                        if d:
                            signal(act, ins, m_icp, g + 1)
                        else:
                            line.free(ins)
                    if s == 1:
                        split_hi(b[1])
                    if s not in (3, 7):
                        gate_unit(s if s < 3 else s - 1)
                    if s == 5:
                        split_hi(b[1].ahead(1))
                    if s > NT // 2:
                        squares(s - 1)
                act.wait_ge(m_o_ld, j * 16 + 16)
                signal(act, act.activation(mo[:], mo[:], ACT.Sigmoid), m_og, j + 1)
                squares(NT - 1)
                gate_unit(6)
                act.wait_ge(m_yt, j + 1)
                staged = mo[:].rearrange("p c n -> p (c n)").rearrange("p (k t) -> p k t", k=2)
                for k in range(2):
                    ins = act.activation(staged[:, k], psw[:, 2048 + k * D:2048 + (k + 1) * D], ACT.Copy, scale=gcol[:, k:k + 1])
                    if k:
                        signal(act, ins, m_ytc, j + 1)
                    else:
                        line.free(ins)
                act.dma_start(yT_d[at(rowy, BC), :].rearrange("(k p) t -> p k t", p=P), staged).then_inc(m_st, 16)
                gate_unit(7)

            ml_act(0, 0)
            with act.Fori(1, ML_HEADS) as j:
                ml_act(j, 2)
            if stop <= 3:
                act.wait_ge(m_st, 64)
                act.wait_ge(st[0], 16 * 37)
                act.wait_ge(st[1], 16 * 36)
                return

            def operand_hi(o, hi, k):
                act.wait_ge(op_ld[o % 2], 16 * (o // 2 + 1))
                signal(act, act.activation(hi[:, k], gt[:, o % 2], ACT.Copy), op_hi, o + 1)
            act.wait_ge(unit_done, Blk(B_GATE + 7).unit(3))
            for k in range(KT):
                operand_hi(k, a_hi, k)
            for k in range(KT):
                operand_hi(KT + k, b_hi, k)
            q = 0
            for n in range(8):
                split_hi(Blk(B_BRANCH + n + 1))
                for c in range(2):
                    act.wait_ge(gt_ld[q % 2], 16 * (q // 2 + 1))
                    signal(act, act.activation(gt[:, q % 2], gt[:, q % 2], ACT.Sigmoid), gt_sig, q + 1)
                    if n == 0:
                        act.wait_ge(st[c], 16 * (37 - c))
                    else:
                        act.wait_ge(br_done, q - 1)
                    unit_out(Blk(B_BRANCH + n), 2 * c)
                    unit_out(Blk(B_BRANCH + n), 2 * c + 1)
                    if n % 2:
                        act.wait_ge(br_done, q + 1)
                        r = (n // 2) * BC + c * P
                        act.dma_start(mergedT[r:r + P, :], mg[:, c]).then_inc(br_st[c], 16)
                    q += 1

            def natural_out(b0, q0, dst):
                q = q0
                for n in range(4):
                    split_hi(Blk(b0 + n + 1))
                    for c in range(2):
                        if q >= 2:
                            act.wait_ge(res_done, q - 1)
                        unit_out(Blk(b0 + n), 2 * c)
                        unit_out(Blk(b0 + n), 2 * c + 1)
                        act.wait_ge(res_done, q + 1)
                        act.dma_start(dst[c * 512:(c + 1) * 512, n * BC:(n + 1) * BC].rearrange("(j p) n -> p j n", p=P),
                                      mg[:, c].rearrange("p (j n) -> p j n", n=BC)).then_inc(res_st[c], 16)
                        q += 1

            for k in range(KT):
                operand_hi(2 * KT + k, a_hi, k)
            natural_out(B_OUT, 0, x2_d)

            def norm_act(w0):
                norm_sq(w0, na)
                for t in range(NT):
                    if t + 1 < NT:
                        norm_sq(w0 + t + 1, na)
                    norm_hi(w0 + t, t, b_hi)
            norm_act(10)

            for j in range(X_HEADS):
                split_hi(Blk(B_Q + j + 1))
                for u in range(4):
                    if j:
                        act.wait_ge(a_sc, 8 * j)
                    unit_out(Blk(B_Q + j), u)
                for t in range(NT + 1):
                    r = 8 * j + t
                    if t < NT:
                        act.wait_ge(a_mx, r + 1)
                        if r >= 2:
                            act.wait_ge(a_tr, r - 1)
                        signal(act, act.activation(pr[:, r % 2], ps[:, 4 + r % 2, 0:M], ACT.Exp, bias=mx[:, r % 2, 1:2],
                                                   scale=BC ** -0.5, accum_out=mx[:, r % 2, 2:3]), a_exp, r + 1)
                    if t >= 1:
                        act.wait_ge(a_tr, r)
                        if j and t == 1:
                            act.wait_ge(a_att, j)
                        signal(act, act.activation(PT[:, :, (t - 1) * P:t * P],
                                                   ps[:, 6 + (r - 1) % 2, 0:M].rearrange("p (c t) -> p c t", c=2),
                                                   ACT.Copy), a_pt, r)
                act.wait_ge(a_att, j + 1)
                if j:
                    act.wait_ge(a_st, 16 * j)
                signal(act, act.activation(atS[:].rearrange("p d t -> p (d t)"), psw[:, 2048:4096], ACT.Copy), a_ev, j + 1)
                act.dma_start(attT_d[j * BC:(j + 1) * BC, :].rearrange("(d p) t -> p d t", p=P), atS[:]).then_inc(a_st, 16)
            for k in range(KT):
                operand_hi(3 * KT + k, a_hi, k)
            natural_out(B_O, 8, x3_d)
            norm_act(18)

            for n, (kind, g) in enumerate(FORDER):
                if kind == "down":
                    continue
                if n + 1 < len(FORDER):
                    split_hi(Blk(B_FF + n + 1))
                for u in range(4):
                    act.wait_ge(unit_done, ff_unit(kind, g, u))
                    if kind == "a" and g:
                        act.wait_ge(f_mul, g)
                    elif kind == "a":
                        act.wait_ge(res_done, 16)
                    else:
                        act.wait_ge(f_conv, 2 * g + 1 + u // 2)
                    signal(act, act.activation(ev[:, u], ps[:, u], ACT.Copy), ev_done, ff_unit(kind, g, u))
                if kind == "a":
                    act.wait_ge(f_conv, 2 * g + 2)
                    signal(act, act.activation(ga[:], ga[:], ACT.Gelu_apprx_tanh), f_gelu, g + 1)
                else:
                    if FORDER[n + 1][0] == "down" and n + 2 < len(FORDER):
                        split_hi(Blk(B_FF + n + 2))
                    act.wait_ge(f_mul, g + 1)
                    if g:
                        act.wait_ge(f_dn, 16 * g)
                    signal(act, act.activation(h_hi[:], ga[:], ACT.Copy), f_hi, g + 1)
            for t in range(NT):
                act.wait_ge(f_acc, 16 * (NFF - 1) + 2 * t + 2)
                signal(act, act.activation(ga[:, t % 2], acc[:, t], ACT.Square, accum_out=ss[:, 1, t:t + 1]), fin_sq, t + 1)
            for t in range(NT):
                act.wait_ge(fin_mul, t + 1)
                act.dma_start(out[0, t * P:(t + 1) * P, :], acc[:, t]).then_inc(fin_st, 16)
            act.wait_ge(fin_st, 16 * NT)

        @block.vector
        def _(dve):
            line = Line(dve, dve_line)

            def split_lo(b):
                dve.wait_ge(w_hi, b.count())
                signal(dve, dve.tensor_tensor(wlo[:, b.slot], w4[:, b.slot], whi[:, b.slot], ALU.subtract), w_lo, b.count())

            def norm_mul(w, bufs):
                dve.wait_ge(n_rs, w + 1)
                if w in (0, 2):
                    dve.wait_ge(g_ld, 16 if w == 0 else 32)
                if w in (10, 18):
                    dve.wait_ge(g2_ld, 16 if w == 10 else 32)
                if w >= 2:
                    dve.wait_ge(n_tr, w - 1)
                signal(dve, dve.scalar_tensor_tensor(bufs["xn"][:, w % 2], bufs["xt"][:, w % 2], rstd[:, 0, w % 2:w % 2 + 1],
                                                     bufs["gb"][:], ALU.mult, ALU.mult), n_mul, w + 1)

            def norm_lo(w, t, hi, lo):
                dve.wait_ge(n_hi, w + 1)
                b0 = (4 + 2 * (w % 2)) * 512
                signal(dve, dve.tensor_tensor(lo[:, :, t * P:(t + 1) * P], psw[:, b0:b0 + D].rearrange("p (k t) -> p k t", k=KT),
                                              hi[:, :, t * P:(t + 1) * P], ALU.subtract), n_lo, w + 1)

            norm_mul(0, nb)
            for w, (name, t) in enumerate(NORM0):
                if w + 1 < len(NORM0):
                    norm_mul(w + 1, nb)
                if w == 2:
                    split_lo(Blk(0))
                    split_lo(Blk(1))
                if w >= 2:
                    split_lo(Blk(w))
                norm_lo(w, t, a_hi, a_lo)
            dve.wait_ge(const_ld, 112)
            dve.wait_ge(param_ld, 144)
            line(dve.tensor_copy(lmask[:], lmask_f[:]))
            dve.wait_ge(col_ready, 1)
            signal(dve, dve.tensor_tensor(lb_raw[:, :, 1], lb_raw[:, :, 0], lb_raw[:, :, 1], ALU.subtract), col_done, 1)
            for k in range(4):
                split_lo(Blk(B_HGT + k + 1))
                if k == 0:
                    dve.wait_ge(grow_ld, 64)
                    for d in range(2):
                        r = slice(BWD * d, BWD * d + 4)
                        line.free(dve.tensor_scalar(gi[r], gi[r], gate_bias[r, 0:1], None, ALU.add))
                        line(dve.tensor_scalar(gf[r], gf[r], gate_bias[r, 1:2], None, ALU.add))
                    signal(dve, dve.scalar_tensor_tensor(gw[:, 0], gf[:], -1.0, gf[:], ALU.mult, ALU.min), grow_dve, 1)
                if k == 1:
                    dve.wait_ge(grow_act, 1)
                    line(dve.scalar_tensor_tensor(gf[:], gf[:], 0.0, gw[:, 1], ALU.min, ALU.subtract))
                    F_, B_ = slice(0, 4), slice(BWD, BWD + 4)
                    line.free(dve.tensor_tensor_scan(gm[F_], gf[F_], gi[F_], 0.0, ALU.add, ALU.max))
                    line.free(dve.tensor_tensor_scan(gm[B_, ::-1], gf[B_, ::-1], gi[B_, ::-1], 0.0, ALU.add, ALU.max))
                    line.free(dve.tensor_tensor_scan(gbc[F_], greset[F_], gf[F_], 0.0, ALU.mult, ALU.add))
                    line(dve.tensor_tensor_scan(gbc[B_, ::-1], greset[B_, ::-1], gf[B_, ::-1], 0.0, ALU.mult, ALU.add))
                    line(dve.tensor_tensor(gi[:], gi[:], gbc[:], ALU.subtract))
                    line(dve.tensor_tensor(gbc[:], gbc[:], gm[:], ALU.subtract))
                    line.free(dve.tensor_copy(gms[F_, 1:NT], gm[F_, P - 1:T - P:P]))
                    line.free(dve.tensor_copy(gms[B_, 0:NT - 1], gm[B_, P::P]))
                    line.free(dve.tensor_copy(gre[F_], gbc[F_, P - 1::P]))
                    line(dve.tensor_copy(gre[B_], gbc[B_, 0::P]))
                    c3 = lambda a: a.rearrange("p (c t) -> p c t", c=NT)
                    bc = lambda a: a[:].rearrange("p (c o) -> p c o", o=1).to_broadcast([ROWS, NT, P])
                    line.free(dve.tensor_tensor(c3(gw[:, 0]), c3(gbc[:]), bc(gms), ALU.add))
                    line.free(dve.tensor_tensor(c3(gw[:, 2]), c3(gi[:]), bc(gre), ALU.add))
                    line.free(dve.tensor_scalar(gw[:, 1], gm[:], -1.0, None, ALU.mult))
                    signal(dve, dve.tensor_tensor(gdec[:], gre[:], gms[:], ALU.add), grow_dve, 2)
                if k == 2:
                    dve.wait_ge(grow_act, 2)
                    signal(dve, dve.tensor_tensor(gds[:], gdec[:].rearrange("p (c o) -> p c o", o=1).to_broadcast([ROWS, NT, 8]),
                                                  sel8[:].rearrange("p (o h) -> p o h", o=1).to_broadcast([ROWS, NT, 8]), ALU.mult),
                           grow_dve, 3)
            with dve.Fori(2, 6) as i:
                for j in range(2):
                    split_lo(Blk(B_HGT + j + 1, i, 2))
            with dve.Fori(0, 4) as i:
                for j in range(2):
                    split_lo(Blk(B_HGN + j + 1, i, 2))

            def conv(x_, y_, w_, k):
                if k == 0:
                    return dve.tensor_scalar(y_[:, 0:T], x_[:, 0:T], w_[1], w_[3], ALU.mult, ALU.add)
                if k == 1:
                    return dve.scalar_tensor_tensor(y_[:, 1:T], x_[:, 0:T - 1], w_[0], y_[:, 1:T], ALU.mult, ALU.add)
                return dve.scalar_tensor_tensor(y_[:, 0:T - 1], x_[:, 1:T], w_[2], y_[:, 0:T - 1], ALU.mult, ALU.add)

            lvl = lambda l: (fkd, 0) if l == 0 else (tot, level_tot(l))

            def hg_start(h):
                line.free(dve.tensor_copy(lb_h[:, 0], lb[:, :, at(h, 1)].rearrange("p d o -> p (d o)")))
                line(dve.tensor_copy(lb_h[:, 1], lb_rest[:, :, at(h, 1)].rearrange("p d o -> p (d o)")))
                dve.wait_ge(h_sgate, h + 1)
                for d in range(2):
                    line(dve.tensor_scalar(fkd[:, d], qfb[:, 2 - d], lb_h[:, 1, 1 - d:2 - d], lb_h[:, 0, 1 - d:2 - d], ALU.mult, ALU.add))
                for d in range(2):
                    line(dve.tensor_scalar(Y[:, d], fkd[:, 1 - d], -1.0, 1.0, ALU.mult, ALU.add))
                for l in range(LEVELS):
                    (a, o), n = lvl(l), T >> l
                    ins = dve.tensor_tensor(view(tot, level_tot(l + 1), [1, n]), view(a, o, [2, n]), view(a, o + 1, [2, n]), ALU.mult)
                    if l < LEVELS - 1:
                        line(ins)
                    else:
                        signal(dve, ins, h_keys, h + 1)

            def key_sums(h):
                signal(dve, dve.tensor_tensor(Sall[:, 0].rearrange("p c v -> p (c v)"), Y[:, 0], Y[:, 1], ALU.add), h_ksum, h + 1)

            def hg_dve(h, step, last=False):
                line.restart()
                bT, bN = Blk(B_ML, h, step), Blk(B_ML + 1, h, step)
                dve.wait_ge(h_sig, h + 1)
                signal(dve, dve.tensor_tensor(qs[:], qs[:], qfb[:, 0], ALU.mult), h_q, h + 1)
                signal(dve, dve.tensor_tensor(X[:], fkd[:], qs[:].rearrange("p (o t) -> p o t", o=1).to_broadcast([P, 2, T]), ALU.mult),
                       h_init, h + 1)
                if step:
                    dve.wait_ge(h_ytc, h)
                line.free(dve.tensor_copy(gcol[:, 0:1], hg_g[:, at(h, 1)]))
                f2 = dve.snap(h * 2) if step else 0
                line.free(dve.tensor_copy(cw[:, :, 0:3].rearrange("p c w -> p w c"), mcw[:, :, at(f2, 2)]))
                line(dve.tensor_copy(cw[:, :, 3:4].rearrange("p c w -> p (c w)"), mcb[:, at(f2, 2)]))
                split_lo(bN)

                def update(l):
                    hh, (a, o), nb_ = 1 << l, lvl(l), T >> l
                    dims = ([T + hh, 2], [2 * hh, nb_ // 2], [1, hh])
                    dve.wait_ge(h_yc, h * LEVELS + l + 1)
                    signal(dve, dve.tensor_tensor(view(Y, 0, *dims), view(Y, 0, *dims),
                                                  view(a, o + nb_ + 1, [-nb_ - 1, 2], [2, nb_ // 2], [0, hh]), ALU.mult),
                           h_updy, h * LEVELS + l + 1)
                    dve.wait_ge(h_lv, h * 8 + l + 2)
                    dve.tensor_tensor(view(X, 0, *dims), view(X, 0, *dims),
                                      view(a, o + 1, [nb_ - 1, 2], [2, nb_ // 2], [0, hh]), ALU.mult).then_inc(h_upd, 1)
                def qk_conv(c, k):
                    if k == 0:
                        dve.wait_ge(ev_done, bT.unit(2 * c + 1))
                        if c or step:
                            dve.wait_ge(conv_st, h * 32 + 16 * c)
                    ins = conv(ev[:].rearrange("p u n -> p (u n)")[:, c * T:(c + 1) * T], cv, [cw[:, c, i:i + 1] for i in range(4)], k)
                    if k < 2:
                        line(ins)
                    else:
                        signal(dve, ins, conv_rd, h * 2 + 1 + c)
                for l in range(LEVELS):
                    update(l)
                    b0 = 2048 + ((l + 1) % 2) * D
                    dve.wait_ge(col_ready, 1)
                    if l == 0:
                        dve.wait_ge(h_diag, h + 1)
                    signal(dve, dve.copy_predicated(Am[:], lmask[:, l:l + 1].to_broadcast([P, NT, P]),
                                                    psw[:, b0:b0 + D].rearrange("p (c t) -> p c t", c=NT)),
                           h_pred, h * LEVELS + l + 1)
                    dve.wait_ge(h_upd, h * LEVELS + l + 1)
                    if 3 <= l <= 5:
                        qk_conv(0, l - 3)
                for k in range(3):
                    qk_conv(1, k)
                split_lo(bN.ahead(1))
                o = level_tot(LEVELS)
                U = lambda d, c: psw[:, 2048 + d * D + c * P:2048 + d * D + (c + 1) * P]
                dve.wait_ge(h_u, h * 2 + 1)
                line(dve.tensor_copy(Sall[:, 0, 1], U(0, 0)))
                dve.wait_ge(h_u, h * 2 + 2)
                line(dve.tensor_copy(Sall[:, 1, NT - 2], U(1, NT - 1)))
                for k in range(1, NT - 1):
                    line.free(dve.scalar_tensor_tensor(Sall[:, 0, k + 1], Sall[:, 0, k], tot[:, o + NT + k:o + NT + k + 1], U(0, k), ALU.mult, ALU.add))
                    c = NT - 1 - k
                    ins = dve.scalar_tensor_tensor(Sall[:, 1, c - 1], Sall[:, 1, c], tot[:, o + c:o + c + 1], U(1, c), ALU.mult, ALU.add)
                    if k < NT - 2:
                        line(ins)
                    else:
                        signal(dve, ins, h_s, h + 1)
                if not last:
                    hg_start(h + 1)
                dve.wait_ge(h_sq, h + 1)
                signal(dve, dve.tensor_reduce(ss[:, 1], Sall[:, 0], AX_X, ALU.add), h_ss, h + 1)
                dve.wait_ge(h_silu, h + 1)
                dve.wait_ge(h_rs, h + 1)
                for c in range(NT):
                    ins = dve.scalar_tensor_tensor(qs[:, c * P:(c + 1) * P], psw[:, 2048 + c * P:2048 + (c + 1) * P], rstd[:, 1, c:c + 1],
                                                   gv[:, c], ALU.mult, ALU.mult)
                    if c < NT - 1:
                        line.free(ins)
                    else:
                        signal(dve, ins, h_y, h + 1)
                if not last:
                    key_sums(h + 1)

            hg_start(0)
            key_sums(0)
            hg_dve(0, 0)
            with dve.Fori(1, HG_HEADS - 1) as h:
                hg_dve(h, 2)
            hg_dve(HG_HEADS - 1, 2, True)
            if stop <= 2:
                return

            dve.wait_ge(m_rows_ld, 32)

            def ml_start(j):
                line.free(dve.tensor_copy(hcol[:], cols[:, :, :, :, at(j, 1)].rearrange("p q c d o -> p q c (d o)")))
                line.free(dve.tensor_copy(hdec[:], decb[:, :, :, at(j, 1)].rearrange("p c d o -> p c (d o)")))
                line.free(dve.memset(C[:], 0.0))
                signal(dve, dve.tensor_scalar(rsel[:], rows[:], onehot[:, at(j, 1)], None, ALU.mult), m_sel, j + 1)

            def ml_dve(j, step, last=False):
                line.restart()
                b = [Blk(B_GATE, j, step), Blk(B_GATE + 1, j, step)]
                for s in range(NT):
                    g = j * NT + s
                    cf, cb = s, NT - 1 - s
                    dve.wait_ge(m_sc, g + 1)
                    if s:
                        dve.wait_ge(m_exp, g)
                    signal(dve, dve.scalar_tensor_tensor(Dm[:].rearrange("p d t -> p (d t)"), ps[:, 4, 2 * P:4 * P], 0.0,
                                                         cmask[:].rearrange("p d t -> p (d t)"), ALU.min, ALU.add), m_arg, g + 1)
                    dve.wait_ge(m_exp, g + 1)
                    if s:
                        dve.wait_ge(m_in, g)
                    signal(dve, dve.scalar_tensor_tensor(Pm[:].rearrange("p d t -> p (d t)"), ps[:, 4, 0:2 * P], BC ** -0.5,
                                                         Em[:].rearrange("p d t -> p (d t)"), ALU.mult, ALU.mult), m_p, g + 1)
                    dve.wait_ge(m_in, g + 1)
                    step_c = 2 * (cb - cf) + 1
                    line(dve.tensor_tensor(den[:, 0], ps[:, 6, 0:2], view(hcol, 2 * cf, [step_c, 2]), ALU.mult))
                    line(dve.tensor_tensor(den[:, 1], den[:, 0], ps[:, 6, 2:4], ALU.add))
                    line(dve.scalar_tensor_tensor(den[:, 2], den[:, 1], -1.0, den[:, 1], ALU.mult, ALU.max))
                    line(dve.tensor_tensor(den[:, 0], den[:, 2], view(hcol, 2 * NT + 2 * cf, [step_c, 2]), ALU.max))
                    line(dve.reciprocal(den[:, 3], den[:, 0]))
                    for d, c in ((0, cf), (1, cb)):
                        line.free(dve.scalar_tensor_tensor(C[:, d, :, BC:BC + 1], C[:, d, :, BC:BC + 1], hdec[:, c, d:d + 1],
                                                           ps[:, 6, 4 + 2 * d:6 + 2 * d].rearrange("p (k n) -> p k n", k=2), ALU.mult, ALU.add))
                    dve.wait_ge(m_icp, g + 1)
                    line(dve.tensor_tensor(num[:].rearrange("p d n -> p (d n)"), inter[:].rearrange("p d n -> p (d n)"), ps[:, 7], ALU.add))
                    for d, c in ((0, cf), (1, cb)):
                        if s < NT // 2:
                            ins = dve.tensor_scalar(Hm[:, c], num[:, d], den[:, 3, d:d + 1], None, ALU.mult)
                        else:
                            ins = dve.scalar_tensor_tensor(Hm[:, c], num[:, d], den[:, 3, d:d + 1], Hm[:, c], ALU.mult, ALU.add)
                        if d:
                            signal(dve, ins, m_hm, g + 1)
                        else:
                            line.free(ins)
                    for d, c, done, sg in ((0, cf, m_upf, m_cf), (1, cb, m_upb, m_cb)):
                        dve.wait_ge(done, g + 1)
                        signal(dve, dve.scalar_tensor_tensor(C[:, d, :, 0:BC], C[:, d, :, 0:BC], hdec[:, c, d:d + 1],
                                                             ps[:, 4 + d].rearrange("p (k n) -> p k n", k=2), ALU.mult, ALU.add), sg, g + 1)
                    if s == 1:
                        split_lo(b[1])
                        if step:
                            dve.wait_ge(m_ytc, j)
                        f2 = dve.snap(j * 2) if step else 0
                        line(dve.tensor_copy(gcol[:], ml_g[:, at(f2, 2)]))
                    if s == 5:
                        split_lo(b[1].ahead(1))
                if not last:
                    ml_start(j + 1)
                dve.wait_ge(m_og, j + 1)
                dve.wait_ge(m_rs, j + 1)
                for c in range(NT):
                    ins = dve.scalar_tensor_tensor(Hm[:, c], Hm[:, c], rstd[:, 1, c:c + 1], mo[:, c], ALU.mult, ALU.mult)
                    if c < NT - 1:
                        line.free(ins)
                    else:
                        signal(dve, ins, m_y, j + 1)

            ml_start(0)
            ml_dve(0, 0)
            with dve.Fori(1, ML_HEADS - 1) as j:
                ml_dve(j, 2)
            ml_dve(ML_HEADS - 1, 2, True)
            if stop <= 3:
                return

            def operand_lo(o, hi, lo, k):
                dve.wait_ge(op_hi, o + 1)
                signal(dve, dve.tensor_tensor(lo[:, k], gt[:, o % 2], hi[:, k], ALU.subtract), op_lo, o + 1)
            for k in range(KT):
                operand_lo(k, a_hi, a_lo, k)
            for k in range(KT):
                operand_lo(KT + k, b_hi, b_lo, k)
            q = 0
            for n in range(8):
                split_lo(Blk(B_BRANCH + n + 1))
                for c in range(2):
                    dve.wait_ge(gt_sig, q + 1)
                    dve.wait_ge(ev_done, Blk(B_BRANCH + n).unit(2 * c + 1))
                    e = ev[:, 2 * c:2 * c + 2].rearrange("p u n -> p (u n)")
                    if n % 2 == 0:
                        if n >= 2:
                            dve.wait_ge(br_st[c], 16 * (n // 2))
                        signal(dve, dve.tensor_tensor(mg[:, c], e, gt[:, q % 2], ALU.mult), br_done, q + 1)
                    else:
                        line(dve.tensor_tensor(gt[:, q % 2], e, gt[:, q % 2], ALU.mult))
                        signal(dve, dve.tensor_tensor(mg[:, c], mg[:, c], gt[:, q % 2], ALU.add), br_done, q + 1)
                    q += 1

            def natural_add(b0, q0):
                q = q0
                for n in range(4):
                    split_lo(Blk(b0 + n + 1))
                    for c in range(2):
                        dve.wait_ge(res_ld[c], 16 * (q // 2 + 1))
                        dve.wait_ge(ev_done, Blk(b0 + n).unit(2 * c + 1))
                        signal(dve, dve.tensor_tensor(mg[:, c], mg[:, c], ev[:, 2 * c:2 * c + 2].rearrange("p u n -> p (u n)"), ALU.add),
                               res_done, q + 1)
                        q += 1

            def norm_dve(w0):
                norm_mul(w0, na)
                for t in range(NT):
                    if t + 1 < NT:
                        norm_mul(w0 + t + 1, na)
                    norm_lo(w0 + t, t, b_hi, b_lo)
            for k in range(KT):
                operand_lo(2 * KT + k, a_hi, a_lo, k)
            natural_add(B_OUT, 0)
            norm_dve(10)
            for j in range(X_HEADS):
                split_lo(Blk(B_Q + j + 1))
                for t in range(NT + 1):
                    r = 8 * j + t
                    if t < NT:
                        dve.wait_ge(a_sc, r + 1)
                        line(dve.reduce_max(mx[:, r % 2, 0:1], ps[:, 4 + r % 2, 0:M], AX_X))
                        signal(dve, dve.tensor_scalar(mx[:, r % 2, 1:2], mx[:, r % 2, 0:1], -BC ** -0.5, None, ALU.mult), a_mx, r + 1)
                    if t >= 1:
                        k = (r - 1) % 2
                        dve.wait_ge(a_exp, r)
                        line(dve.reciprocal(mx[:, k, 2:3], mx[:, k, 2:3]))
                        signal(dve, dve.tensor_scalar(pr[:, k], pr[:, k], mx[:, k, 2:3], None, ALU.mult), a_nrm, r)
            for k in range(KT):
                operand_lo(3 * KT + k, a_hi, a_lo, k)
            natural_add(B_O, 8)
            norm_dve(18)

            def down_adds(g):
                for k in range(16):
                    if g == 0 and k == 0:
                        dve.wait_ge(acc_ld, 32)
                    dve.wait_ge(f_dn, 16 * g + k + 1)
                    a = acc[:, k // 2, (k % 2) * HALF:(k % 2 + 1) * HALF]
                    signal(dve, dve.tensor_tensor(a, a, ps[:, 4 + k % 4], ALU.add), f_acc, 16 * g + k + 1)
            for n, (kind, g) in enumerate(FORDER):
                if n + 1 < len(FORDER):
                    split_lo(Blk(B_FF + n + 1))
                if kind == "a":
                    if g:
                        dve.wait_ge(f_hi, g)
                    for c in range(2):
                        dve.wait_ge(ev_done, ff_unit("a", g, 2 * c + 1))
                        f = 2 * g + c
                        w_ = [fcw[:, k, f:f + 1] for k in range(3)] + [fcb[:, f:f + 1]]
                        for k in range(3):
                            ins = conv(ev[:].rearrange("p u n -> p (u n)")[:, c * T:(c + 1) * T], ga[:, c], w_, k)
                            if k < 2:
                                line(ins)
                            else:
                                signal(dve, ins, f_conv, 2 * g + c + 1)
                elif kind == "b":
                    dve.wait_ge(f_gelu, g + 1)
                    dve.wait_ge(ev_done, ff_unit("b", g, 3))
                    signal(dve, dve.tensor_tensor(ga[:].rearrange("p c t -> p (c t)"), ga[:].rearrange("p c t -> p (c t)"),
                                                  ev[:].rearrange("p u n -> p (u n)"), ALU.mult), f_mul, g + 1)
                    if g == 0:
                        dve.wait_ge(f_hi, 1)
                        signal(dve, dve.tensor_tensor(h_lo[:], ga[:], h_hi[:], ALU.subtract), f_lo, 1)
                else:
                    down_adds(g)
                    if g + 1 < NFF:
                        dve.wait_ge(f_hi, g + 2)
                        signal(dve, dve.tensor_tensor(h_lo[:], ga[:], h_hi[:], ALU.subtract), f_lo, g + 2)
            for t in range(NT):
                dve.wait_ge(fin_rs, t + 1)
                signal(dve, dve.scalar_tensor_tensor(acc[:, t], acc[:, t], rstd[:, 1, t:t + 1], mg[:, 0], ALU.mult, ALU.mult), fin_mul, t + 1)

        @block.tensor
        def _(pe):
            def wait_bank(b, u):
                if b.base == B_HGT and not b.step:
                    pe.wait_ge(ev_done, FIRST_UNITS)
                else:
                    pe.wait_ge(ev_done, b.unit(u, 1))

            def products(o, slot, hi, lo, steps, stationary, moving, last_inc):
                n = len(steps)
                for k, s_ in enumerate(steps):
                    for part, (sw, mw) in enumerate(((0, 0), (0, 1), (1, 0))):
                        ins = pe.matmul(o, stationary(s_, sw), moving(s_, mw), start=k == 0 and part == 0,
                                        stop=k == n - 1 and part == 2)
                return ins

            W = (whi, wlo)

            def half_T(b, u, part, op):
                c, t = u // 2, u % 2
                if part == 0:
                    wait_bank(b, u)
                    if u == 0:
                        pe.wait_ge(w_lo, b.count())
                ks = range(4 * part, 4 * part + 4)
                for k in ks:
                    for q, (sw, mw) in enumerate(((0, 0), (0, 1), (1, 0))):
                        ins = pe.matmul(ps[:, u], W[sw][:, b.slot, k, c * P:(c + 1) * P], op[mw][:, k, t * HALF:(t + 1) * HALF],
                                        start=k == 0 and q == 0, stop=k == KT - 1 and q == 2)
                if part:
                    ins.then_inc(unit_done, 1)

            def half_N(b, u, part, op):
                t = 2 * u + part
                if part == 0:
                    wait_bank(b, u)
                    if u == 0:
                        pe.wait_ge(w_lo, b.count())
                for k in range(KT):
                    for q, (sw, mw) in enumerate(((0, 0), (0, 1), (1, 0))):
                        ins = pe.matmul(ps[:, u, part * BC:(part + 1) * BC], op[sw][:, k, t * P:(t + 1) * P], W[mw][:, b.slot, k],
                                        start=k == 0 and q == 0, stop=k == KT - 1 and q == 2)
                if part:
                    ins.then_inc(unit_done, 1)

            def whole(fn, b, op):
                for u in range(4):
                    fn(b, u, 0, op)
                    fn(b, u, 1, op)

            opA, opB = (a_hi, a_lo), (b_hi, b_lo)

            def norm_tr(w, bufs):
                pe.wait_ge(n_mul, w + 1)
                if w >= 2:
                    pe.wait_ge(n_lo, w - 1)
                b0 = (4 + 2 * (w % 2)) * 512
                for k in range(KT):
                    ins = pe.transpose(psw[:, b0 + k * P:b0 + (k + 1) * P], bufs["xn"][:, w % 2, k * P:(k + 1) * P], ident[:])
                ins.then_inc(n_tr, 1)

            pe.wait_ge(const_ld, 112)
            pe.wait_ge(param_ld, 144)
            pe.wait_ge(ones_done, 1)
            pe.transpose(ps[:, 0, 0:112], prow[0:112, 0], ident[0:112, 0:112])
            pe.transpose(ps[:, 0, P:P + 88], prow[0:88, 1], ident[0:88, 0:88]).then_inc(col_tr, 1)

            def kv(n):
                if n == 0:
                    pe.wait_ge(n_lo, 2)
                    pe.wait_ge(col_ready, 1)
                pe.wait_ge(w_lo, n + 1)
                if n >= 2:
                    pe.wait_ge(ev_done, n - 1)
                for c in range(2):
                    for k in range(KT):
                        for q, (sw, mw) in enumerate(((0, 0), (0, 1), (1, 0))):
                            if n < 4:
                                l_, r_ = W[sw][:, n % 2, k, c * P:(c + 1) * P], opA[mw][:, k, 0:M]
                            else:
                                l_, r_ = opA[sw][:, k, c * P:(c + 1) * P], W[mw][:, n % 2, k]
                            ins = pe.matmul(ps[:, n % 2, c * BC:(c + 1) * BC], l_, r_, start=k == 0 and q == 0, stop=k == KT - 1 and q == 2)
                ins.then_inc(unit_done, 1)

            for w in range(len(NORM0)):
                norm_tr(w, nb)
                if w >= 2:
                    kv(w - 2)
            pe.wait_ge(n_lo, len(NORM0))
            pe.wait_ge(w_lo, KV + 1)
            pe.wait_ge(ev_done, KV)
            for u in range(2):
                for k in range(KT):
                    for q, (sw, mw) in enumerate(((0, 0), (0, 1), (1, 0))):
                        ins = pe.matmul(ps[:, u], W[sw][:, KV % 2, k, 0:P], opA[mw][:, k, u * HALF:(u + 1) * HALF],
                                        start=k == 0 and q == 0, stop=k == KT - 1 and q == 2)
                ins.then_inc(unit_done, 1)
            for k in range(4):
                if k == 3:
                    pe.wait_ge(grow_dve, 3)
                    for q in range(3):
                        for c in range(NT):
                            i = q * NT + c
                            o = (4 + i // 12) * 512 + (i % 12) * ROWS
                            pe.transpose(psw[:, o:o + ROWS], gw[:, q, c * P:(c + 1) * P], ident[0:ROWS, 0:ROWS])
                    pe.matmul(ps[:, 6, 0:64], ones[0:ROWS, :], gds[:].rearrange("p c h -> p (c h)"), start=True, stop=True).then_inc(g_tr, 1)
                whole(half_T, Blk(B_HGT + k), opA)
            with pe.Fori(2, 6) as i:
                for j in range(2):
                    whole(half_T, Blk(B_HGT + j, i, 2), opA)
            with pe.Fori(0, 4) as i:
                for j in range(2):
                    whole(half_N, Blk(B_HGN + j, i, 2), opA)

            def hg_pe(h, step):
                bT, bN = Blk(B_ML, h, step), Blk(B_ML + 1, h, step)
                chunk = lambda t, c: t[:, c * P:(c + 1) * P]
                pair = lambda k, c: psw[:, 2048 + k * D + c * P:2048 + k * D + (c + 1) * P]
                fill = iter([(half_T, bT, u, p) for u in range(4) for p in range(2)] + [(half_N, bN, u, p) for u in range(4) for p in range(2)])

                def dense(n=1):
                    for _ in range(n):
                        f, b, u, p = next(fill)
                        f(b, u, p, opA)
                pe.wait_ge(h_ksum, h + 1)
                pe.wait_ge(h_q, h + 1)
                if step:
                    pe.wait_ge(h_y, h)
                for c in range(NT):
                    ins = pe.matmul(pair(0, c), chunk(Sall[:, 0].rearrange("p c v -> p (c v)"), c), chunk(qs, c), start=True, stop=True)
                ins.then_inc(h_lv, 1)
                dense()
                for l in range(LEVELS):
                    hh = 1 << l
                    if l == 0:
                        pe.wait_ge(h_init, h + 1)
                        if step:
                            pe.wait_ge(h_ytc, h)
                    else:
                        pe.wait_ge(h_upd, h * LEVELS + l)
                        pe.wait_ge(h_diag, h + 1) if l == 1 else pe.wait_ge(h_pred, h * LEVELS + l - 1)
                    pe.wait_ge(h_yc, h * LEVELS + l + 1)
                    dims = ([2 * hh, P // (2 * hh)], [T + hh, 2], [1, hh])
                    for c in range(NT):
                        ins = pe.matmul(pair((l + 1) % 2, c), chunk(Yc, c), view(X, c * P, *dims), start=True, stop=True)
                    ins.then_inc(h_lv, 1)
                    dense()
                pe.wait_ge(h_updy, h * LEVELS + LEVELS)
                pe.wait_ge(h_upd, h * LEVELS + LEVELS)
                for d in range(2):
                    pe.wait_ge(h_pred, h * LEVELS + LEVELS - 1 + d)
                    for c in range(NT):
                        ins = pe.transpose(pair(d, c), Y[:, d, c * P:(c + 1) * P], ident[:])
                    ins.then_inc(h_kdt, 1)
                    dense()
                pe.wait_ge(h_vld, h * 32 + 32)
                for d in range(2):
                    pe.wait_ge(h_kd, h * 2 + 1 + d)
                    for c in range(NT):
                        ins = pe.matmul(pair(d, c), chunk(fkd[:, d], c), vg[:, 0, c], start=True, stop=True)
                    ins.then_inc(h_u, 1)
                dense(2)
                pe.wait_ge(h_s, h + 1)
                for c in range(NT):
                    parts = [(Am[:, c], vg[:, 0, c])]
                    if c:
                        parts.append((X[:, 1, c * P:(c + 1) * P], Sall[:, 0, c]))
                    if c < NT - 1:
                        parts.append((X[:, 0, c * P:(c + 1) * P], Sall[:, 1, c]))
                    for k, (l_, r_) in enumerate(parts):
                        ins = pe.matmul(pair(0, c), l_, r_, start=k == 0, stop=k == len(parts) - 1)
                ins.then_inc(h_o, 1)
                dense(3)
                pe.wait_ge(h_y, h + 1)
                for c in range(NT):
                    ins = pe.transpose(pair(1, c), chunk(qs, c), ident[:])
                ins.then_inc(h_yt, 1)
                dense()

            hg_pe(0, 0)
            with pe.Fori(1, HG_HEADS) as h:
                hg_pe(h, 2)
            if stop <= 2:
                return

            def ml_pe(j, step):
                b = [Blk(B_GATE, j, step), Blk(B_GATE + 1, j, step)]
                fill = iter([(b[k], u, p) for k in range(2) for u in range(4) for p in range(2)])

                def dense(n=1):
                    for _ in range(n):
                        half_T(*next(fill), opA)
                pe.wait_ge(m_qk_ld, j * 32 + 32)
                if step:
                    pe.wait_ge(m_ytc, j)
                else:
                    pe.wait_ge(h_ytc, HG_HEADS)
                    pe.wait_ge(h_y, HG_HEADS)
                for c in range(NT):
                    for k in range(2):
                        o = 2048 + c * BC + k * P
                        ins = pe.transpose(psw[:, o:o + P], mk[:, k, c * P:(c + 1) * P], ident[:])
                ins.then_inc(m_kt, 1)
                dense()
                pe.wait_ge(m_v_ld, j * 16 + 16)
                for s in range(NT):
                    g = j * NT + s
                    cs_ = (s, NT - 1 - s)
                    tok = lambda t, k, c: t[:, k, c * P:(c + 1) * P]
                    if s == 0:
                        pe.wait_ge(m_kn, j + 1)
                        pe.wait_ge(m_sel, j + 1)
                    else:
                        pe.wait_ge(m_cb, g)
                    for d, c in enumerate(cs_):
                        for k in range(2):
                            pe.matmul(ps[:, 4, d * P:(d + 1) * P], tok(mk, k, c), tok(mq, k, c), start=k == 0, stop=k == 1)
                    for d, c in enumerate(cs_):
                        o = (2 + d) * P
                        pe.matmul(ps[:, 4, o:o + P], dirsel[:, d], rsel[:, 0, c * P:(c + 1) * P], start=True, stop=False)
                        ins = pe.matmul(ps[:, 4, o:o + P], rsel[:, 1, c * P:(c + 1) * P], dirsel[:, d], start=False, stop=True)
                    ins.then_inc(m_sc, 1)
                    for d, c in enumerate(cs_):
                        for k in range(2):
                            pe.matmul(ps[:, 5, d * BC:(d + 1) * BC], tok(mq, k, c), C[:, d, k, 0:BC], start=k == 0, stop=k == 1)
                        for k in range(2):
                            ins = pe.matmul(ps[:, 6, d:d + 1], tok(mq, k, c), C[:, d, k, BC:BC + 1], start=k == 0, stop=k == 1)
                    ins.then_inc(m_int, 1)
                    dense()
                    pe.wait_ge(m_kw, g + 1)
                    for d in range(2):
                        for k in range(2):
                            pe.matmul(ps[:, 6, 4 + 2 * d + k:5 + 2 * d + k], kw[:, d, k * P:(k + 1) * P], ones[:, 0:1], start=True, stop=True)
                    pe.wait_ge(m_p, g + 1)
                    for d, c in enumerate(cs_):
                        pe.matmul(ps[:, 7, d * BC:(d + 1) * BC], Pm[:, d], mv[:, c], start=True, stop=True)
                        ins = pe.matmul(ps[:, 6, 2 + d:3 + d], Pm[:, d], ones[:, 0:1], start=True, stop=True)
                    ins.then_inc(m_in, 1)
                    for d, c, done in ((0, cs_[0], m_upf), (1, cs_[1], m_upb)):
                        if d:
                            pe.wait_ge(m_icp, g + 1)
                        for k in range(2):
                            ins = pe.matmul(ps[:, 4 + d, k * BC:(k + 1) * BC], kw[:, d, k * P:(k + 1) * P], mv[:, c], start=True, stop=True)
                        ins.then_inc(done, 1)
                    if s % 2 == 0:
                        dense()
                dense(2)
                pe.wait_ge(m_y, j + 1)
                for k in range(2):
                    for c in range(NT):
                        o = 2048 + k * D + c * P
                        ins = pe.transpose(psw[:, o:o + P], Hm[:, c, k * P:(k + 1) * P], ident[:])
                ins.then_inc(m_yt, 1)
                dense()

            ml_pe(0, 0)
            with pe.Fori(1, ML_HEADS) as j:
                ml_pe(j, 2)
            if stop <= 3:
                return

            pe.wait_ge(op_lo, 2 * KT)
            for n in range(8):
                whole(half_T, Blk(B_BRANCH + n), opB if n % 2 else opA)
            pe.wait_ge(op_lo, 3 * KT)
            for n in range(4):
                whole(half_N, Blk(B_OUT + n), opA)
            for t in range(NT):
                norm_tr(10 + t, na)
            pe.wait_ge(n_lo, 18)
            pe.wait_ge(kx_ld, 32)
            for j in range(X_HEADS):
                b = Blk(B_Q + j)
                if j == 0:
                    whole(half_T, b, opB)
                fill = iter([(Blk(B_Q + j + 1), u, p) for u in range(4) for p in range(2)]) if j + 1 < X_HEADS else iter([])
                for t in range(NT + 1):
                    r = 8 * j + t
                    if t < NT:
                        if t == 0:
                            pe.wait_ge(ev_done, b.unit(3))
                            if j:
                                pe.wait_ge(a_ev, j)
                        if r >= 2:
                            pe.wait_ge(a_exp, r - 1)
                        for k in range(2):
                            ins = pe.matmul(ps[:, 4 + r % 2, 0:M], ev[:].rearrange("p u n -> p (u n)")[:, k * T + t * P:k * T + (t + 1) * P],
                                            kx[:, 2 * j + k], start=k == 0, stop=k == 1)
                        ins.then_inc(a_sc, 1)
                        for f in fill:
                            half_T(*f, opB)
                            break
                    if t >= 1:
                        pe.wait_ge(a_nrm, r)
                        if t >= 3:
                            pe.wait_ge(a_pt, r - 2)
                        for c in range(2):
                            ins = pe.transpose(ps[:, 6 + (r - 1) % 2, c * P:(c + 1) * P], pr[:, (r - 1) % 2, c * P:(c + 1) * P], ident[:])
                        ins.then_inc(a_tr, 1)
                pe.wait_ge(a_pt, 8 * j + 8)
                for d in range(2):
                    for t in range(2):
                        for c in range(2):
                            ins = pe.matmul(ps[:, 4 + 2 * d + t], vx[:, c, j * BC + d * P:j * BC + (d + 1) * P],
                                            PT[:, c, t * HALF:(t + 1) * HALF], start=c == 0, stop=c == 1)
                ins.then_inc(a_att, 1)
            pe.wait_ge(op_lo, 4 * KT)
            for n in range(4):
                whole(half_N, Blk(B_O + n), opA)
            for t in range(NT):
                norm_tr(18 + t, na)
            pe.wait_ge(n_lo, 26)
            wd = [w_[:, :, :, :].rearrange("p s k n -> p s (k n)").rearrange("p s (k n) -> p s k n", k=2) for w_ in W]
            HH = (h_hi, h_lo)
            for n, (kind, g) in enumerate(FORDER):
                slot = (B_FF + n) % 2
                pe.wait_ge(w_lo, B_FF + n + 1)
                if kind != "down":
                    for u in range(4):
                        pe.wait_ge(ev_done, ff_unit(kind, g, u) - 4)
                        for k in range(KT):
                            for q, (sw, mw) in enumerate(((0, 0), (0, 1), (1, 0))):
                                ins = pe.matmul(ps[:, u], W[sw][:, slot, k, (u // 2) * P:(u // 2 + 1) * P],
                                                opB[mw][:, k, (u % 2) * HALF:(u % 2 + 1) * HALF], start=k == 0 and q == 0, stop=k == KT - 1 and q == 2)
                        ins.then_inc(unit_done, 1)
                    continue
                pe.wait_ge(f_lo, g + 1)
                for m in range(16):
                    t, nh = m // 2, m % 2
                    if 16 * g + m >= 4:
                        pe.wait_ge(f_acc, 16 * g + m - 3)
                    for k in range(2):
                        for q, (sw, mw) in enumerate(((0, 0), (0, 1), (1, 0))):
                            ins = pe.matmul(ps[:, 4 + m % 4], HH[sw][:, k, t * P:(t + 1) * P], wd[mw][:, slot, k, nh * HALF:(nh + 1) * HALF],
                                            start=k == 0 and q == 0, stop=k == 1 and q == 2)
                    ins.then_inc(f_dn, 1)




def ff_order():
    order = []
    for g in range(NFF):
        order += [("a", g), ("b", g)]
        if g:
            order.append(("down", g - 1))
    return order + [("down", NFF - 1)]


def ff_unit(kind, g, u):
    return Blk(B_FF + 2 * g + (kind == "b")).unit(u)


_INS = ["x", "mem", "norm_mix_g", "w_in", "ml_conv_w", "ml_conv_b", "ml_gate_b", "ml_norm_g", "hg_lb", "hg_norm_g",
        "w_branch_m", "w_branch_h", "w_out", "norm_x_g", "norm_mem_g", "w_q_x", "w_kv_x", "w_o_x", "norm_ffn_g",
        "w_up", "ffn_conv_w", "ffn_conv_b", "w_down", "norm_final_g"]


def _constants(np):
    i = np.arange(P)
    s, t = i[:, None], i[None, :]
    level = np.stack([(s >> (l + 1) == t >> (l + 1)) & (s >> l != t >> l) for l in range(LEVELS)], 1)
    causal = np.stack([np.where(s <= t, 0.0, -1e30), np.where(s >= t, 0.0, -1e30)], 1)
    reset = np.ones((ROWS, T), np.float32)
    reset[:BWD, ::P] = 0.0
    reset[BWD:, P - 1::P] = 0.0
    onehot = np.zeros((ROWS, ML_HEADS), np.float32)
    sel8 = np.zeros((ROWS, 8), np.float32)
    for j in range(ML_HEADS):
        onehot[j, j] = onehot[BWD + j, j] = 1.0
        sel8[j, j] = sel8[BWD + j, ML_HEADS + j] = 1.0
    dirsel = np.zeros((ROWS, 2, P), np.float32)
    dirsel[:4, 0] = dirsel[BWD:, 1] = 1.0
    return {"c_dirsel": dirsel, "c_ident": np.eye(P, dtype=np.float32), "c_lmask": level.astype(np.float32),
            "c_cmask": causal.astype(np.float32), "c_reset": reset, "c_onehot": onehot, "c_sel8": sel8}


def kernel(**inputs):
    import numpy as _np
    import concourse.bacc as _bacc
    from concourse.bass_utils import run_bass_kernel_spmd as _run

    nc = _bacc.Bacc("TRN2", target_bir_lowering=False, num_devices=1)
    arrays = {n: _np.ascontiguousarray(inputs[n]) for n in _INS}
    arrays.update(_constants(_np))
    aps = {n: nc.dram_tensor(f"in_{n}", a.shape, mybir.dt.from_np(a.dtype), kind="ExternalInput").ap()
           for n, a in arrays.items()}
    out = nc.dram_tensor("out_x", (1, T, D), F32, kind="ExternalOutput").ap()
    build(nc, aps, out)
    r = _run(nc, [{f"in_{n}": a for n, a in arrays.items()}], core_ids=[0])
    return r.results[0]["out_x"]
```
